# Optimizing a Trainium2 kernel written in Bass

```python
import math
import jax, jax.numpy as jnp
from jax import lax
import numpy as np

D_MODEL = 1024
BATCH = 1
SEQ = 256
DEPTH = 2

HEAD_DIM = 64
N_HEADS_A = 8
N_HEADS_B = 8
D_ATTN = (N_HEADS_A + N_HEADS_B) * HEAD_DIM
D_ATTN_IN = 3 * D_ATTN + N_HEADS_B
MOBA_BLOCK = 256
MOBA_TOPK = 3
MOBA_QCHUNK = 32
FOX_QBLOCK = 128
REL_BUCKETS = 32
REL_MAX_DIST = 128
SGU_CHUNK = 128
SGU_GROUPS = 8
SGU_WIDTH = D_MODEL
D_FF = 2816
PLE_DIM = 256
N_EVEN = (DEPTH + 1) // 2
N_ODD = DEPTH // 2
DN_ALPHA = (2.0 * DEPTH) ** 0.25
DN_BETA = (8.0 * DEPTH) ** -0.25
LN_EPS = 1e-5
NEG_INF = -1e30

kernel_name = "hybrid_moba_fox_gmlp_macaron_deepnorm"

def layer_norm(x, g, b):
    xf = x.astype(jnp.float32)
    mu = jnp.mean(xf, axis=-1, keepdims=True)
    var = jnp.mean(jnp.square(xf - mu), axis=-1, keepdims=True)
    y = (xf - mu) * lax.rsqrt(var + LN_EPS)
    return (y * g.astype(jnp.float32) + b.astype(jnp.float32)).astype(x.dtype)

def swiglu(x, w_gate, w_up, w_down):
    return (jax.nn.silu(x @ w_gate) * (x @ w_up)) @ w_down

def t5_bucket(n):
    n = jnp.maximum(n, 0)
    max_exact = REL_BUCKETS // 2
    nf = jnp.maximum(n, max_exact).astype(jnp.float32)
    large = max_exact + (jnp.log(nf / max_exact) / math.log(REL_MAX_DIST / max_exact)
                         * (REL_BUCKETS - max_exact)).astype(jnp.int32)
    large = jnp.minimum(large, REL_BUCKETS - 1)
    return jnp.where(n < max_exact, n, large)

def moba_attention(q, k, v, rel_bias):
    B, H, S, hd = q.shape
    nb = -(-S // MOBA_BLOCK)
    sp = nb * MOBA_BLOCK
    pad = ((0, 0), (0, 0), (0, sp - S), (0, 0))
    q, k, v = jnp.pad(q, pad), jnp.pad(k, pad), jnp.pad(v, pad)
    kb = k.reshape(B, H, nb, MOBA_BLOCK, hd)
    vb = v.reshape(B, H, nb, MOBA_BLOCK, hd)
    kbar = jnp.mean(kb.astype(jnp.float32), axis=3).astype(k.dtype)
    topk = min(MOBA_TOPK, nb)
    tbl = rel_bias.T.astype(jnp.float32)
    bi = jnp.arange(B)[:, None, None, None]
    hi = jnp.arange(H)[None, :, None, None]
    r = jnp.arange(MOBA_BLOCK)
    scale = hd ** -0.5
    nsel = topk * MOBA_BLOCK

    def chunk(c):
        start = c * MOBA_QCHUNK
        blk = start // MOBA_BLOCK
        qc = lax.dynamic_slice_in_dim(q, start, MOBA_QCHUNK, axis=2)
        t = start + jnp.arange(MOBA_QCHUNK)
        gate = jnp.einsum('bhqd,bhnd->bhqn', qc, kbar).astype(jnp.float32)
        gate = jnp.where(jnp.arange(nb) < blk, gate, NEG_INF)
        _, idx = lax.top_k(gate, topk)
        valid = jnp.arange(topk) < blk
        kg = kb[bi, hi, idx]
        vg = vb[bi, hi, idx]
        s_sel = jnp.einsum('bhqd,bhqkrd->bhqkr', qc, kg).astype(jnp.float32) * scale
        pos_sel = idx[..., None] * MOBA_BLOCK + r
        s_sel = s_sel + tbl[hi[..., None], t5_bucket(t[:, None, None] - pos_sel)]
        s_sel = jnp.where(valid[:, None], s_sel, NEG_INF)
        k_own = lax.dynamic_slice_in_dim(kb, blk, 1, axis=2)[:, :, 0]
        v_own = lax.dynamic_slice_in_dim(vb, blk, 1, axis=2)[:, :, 0]
        rel_own = t[:, None] - (blk * MOBA_BLOCK + r)[None, :]
        s_own = (jnp.einsum('bhqd,bhrd->bhqr', qc, k_own).astype(jnp.float32) * scale
                 + tbl[:, t5_bucket(rel_own)])
        s_own = jnp.where(rel_own >= 0, s_own, NEG_INF)
        logits = jnp.concatenate([s_sel.reshape(B, H, MOBA_QCHUNK, nsel), s_own], axis=-1)
        prob = jax.nn.softmax(logits, axis=-1).astype(v.dtype)
        p_sel = prob[..., :nsel].reshape(B, H, MOBA_QCHUNK, topk, MOBA_BLOCK)
        return (jnp.einsum('bhqkr,bhqkrd->bhqd', p_sel, vg)
                + jnp.einsum('bhqr,bhrd->bhqd', prob[..., nsel:], v_own))

    out = lax.map(chunk, jnp.arange(sp // MOBA_QCHUNK))
    return jnp.moveaxis(out, 0, 2).reshape(B, H, sp, hd)[:, :, :S]

def forgetting_attention(q, k, v, log_f):
    B, H, S, hd = q.shape
    c = jnp.cumsum(log_f, axis=-1)
    scale = hd ** -0.5
    s_pos = jnp.arange(S)

    def block(i):
        start = i * FOX_QBLOCK
        qb = lax.dynamic_slice_in_dim(q, start, FOX_QBLOCK, axis=2)
        cb = lax.dynamic_slice_in_dim(c, start, FOX_QBLOCK, axis=2)
        t = start + jnp.arange(FOX_QBLOCK)
        logits = (jnp.einsum('bhqd,bhsd->bhqs', qb, k).astype(jnp.float32) * scale
                  + (cb[..., None] - c[:, :, None, :]))
        logits = jnp.where(t[:, None] >= s_pos[None, :], logits, NEG_INF)
        prob = jax.nn.softmax(logits, axis=-1).astype(v.dtype)
        return jnp.einsum('bhqs,bhsd->bhqd', prob, v)

    out = lax.map(block, jnp.arange(S // FOX_QBLOCK))
    return jnp.moveaxis(out, 0, 2).reshape(B, H, S, hd)

def mixer_attention(x, w_in, b_f, w_out, rel_bias):
    B, S, _ = x.shape
    h = x @ w_in
    wa = N_HEADS_A * HEAD_DIM
    wb = N_HEADS_B * HEAD_DIM
    qkv_a = h[..., :3 * wa].reshape(B, S, 3, N_HEADS_A, HEAD_DIM).transpose(2, 0, 3, 1, 4)
    qkv_b = h[..., 3 * wa:3 * wa + 3 * wb].reshape(B, S, 3, N_HEADS_B, HEAD_DIM).transpose(2, 0, 3, 1, 4)
    f_logit = (h[..., 3 * wa + 3 * wb:] + b_f).astype(jnp.float32)
    log_f = jax.nn.log_sigmoid(f_logit).transpose(0, 2, 1)
    o_a = moba_attention(qkv_a[0], qkv_a[1], qkv_a[2], rel_bias)
    o_b = forgetting_attention(qkv_b[0], qkv_b[1], qkv_b[2], log_f)
    o = jnp.concatenate([o_a, o_b], axis=1).transpose(0, 2, 1, 3).reshape(B, S, D_ATTN)
    return o @ w_out

def mixer_sgu(x, w_in, b_in, ln_g, ln_b, w_s, b_s, w_out):
    B, S, _ = x.shape
    h = jax.nn.gelu(x @ w_in + b_in)
    u, v = jnp.split(h, 2, axis=-1)
    v = layer_norm(v, ln_g, ln_b)
    nc = S // SGU_CHUNK
    gw = SGU_WIDTH // SGU_GROUPS
    v = v.reshape(B, nc, SGU_CHUNK, SGU_GROUPS, gw)
    causal = jnp.tril(jnp.ones((SGU_CHUNK, SGU_CHUNK), dtype=bool))
    w = jnp.where(causal, w_s, 0)
    mixed = jnp.einsum('gts,bcsgd->bctgd', w, v) + b_s.T[None, None, :, :, None]
    y = u * mixed.reshape(B, S, SGU_WIDTH)
    return y @ w_out

def setup_inputs(seed: int = 0) -> dict:
    key = jax.random.key(seed)
    ks = jax.random.split(key, 20)
    D = D_MODEL

    def nrm(k, shape, s):
        return jax.random.normal(k, shape, jnp.float32) * s

    return {
        "x": nrm(ks[0], (BATCH, SEQ, D), 1.0),
        "p": nrm(ks[1], (DEPTH, BATCH, SEQ, PLE_DIM), 1.0),
        "ln_g": 1.0 + nrm(ks[2], (DEPTH, 3, D), 0.02),
        "ln_b": nrm(ks[3], (DEPTH, 3, D), 0.02),
        "ffn_w_gate": nrm(ks[4], (DEPTH, 2, D, D_FF), D ** -0.5),
        "ffn_w_up": nrm(ks[5], (DEPTH, 2, D, D_FF), D ** -0.5),
        "ffn_w_down": nrm(ks[6], (DEPTH, 2, D_FF, D), DN_BETA * D_FF ** -0.5),
        "attn_w_in": nrm(ks[7], (N_EVEN, D, D_ATTN_IN), D ** -0.5),
        "attn_b_f": jax.random.uniform(ks[8], (N_EVEN, N_HEADS_B), jnp.float32, 2.0, 6.0),
        "attn_w_out": nrm(ks[9], (N_EVEN, D_ATTN, D), DN_BETA * D_ATTN ** -0.5),
        "rel_bias": nrm(ks[10], (REL_BUCKETS, N_HEADS_A), 0.5),
        "sgu_w_in": nrm(ks[11], (N_ODD, D, 2 * SGU_WIDTH), D ** -0.5),
        "sgu_b_in": nrm(ks[12], (N_ODD, 2 * SGU_WIDTH), 0.02),
        "sgu_ln_g": 1.0 + nrm(ks[13], (N_ODD, SGU_WIDTH), 0.02),
        "sgu_ln_b": nrm(ks[14], (N_ODD, SGU_WIDTH), 0.02),
        "sgu_w_s": nrm(ks[15], (N_ODD, SGU_GROUPS, SGU_CHUNK, SGU_CHUNK), SGU_CHUNK ** -0.5),
        "sgu_b_s": 1.0 + nrm(ks[16], (N_ODD, SGU_GROUPS, SGU_CHUNK), 0.1),
        "sgu_w_out": nrm(ks[17], (N_ODD, SGU_WIDTH, D), DN_BETA * SGU_WIDTH ** -0.5),
        "ple_w_proj": nrm(ks[18], (DEPTH, PLE_DIM, D), PLE_DIM ** -0.5),
        "ple_w_gate": nrm(ks[19], (DEPTH, D, D), D ** -0.5),
    }

def reference(x, p, ln_g, ln_b, ffn_w_gate, ffn_w_up, ffn_w_down, attn_w_in, attn_b_f,
              attn_w_out, rel_bias, sgu_w_in, sgu_b_in, sgu_ln_g, sgu_ln_b, sgu_w_s, sgu_b_s,
              sgu_w_out, ple_w_proj, ple_w_gate):
    for i in range(DEPTH):
        j = i // 2
        x = layer_norm(DN_ALPHA * x + 0.5 * swiglu(x, ffn_w_gate[i, 0], ffn_w_up[i, 0], ffn_w_down[i, 0]),
                       ln_g[i, 0], ln_b[i, 0])
        if i % 2 == 0:
            m = mixer_attention(x, attn_w_in[j], attn_b_f[j], attn_w_out[j], rel_bias)
        else:
            m = mixer_sgu(x, sgu_w_in[j], sgu_b_in[j], sgu_ln_g[j], sgu_ln_b[j],
                          sgu_w_s[j], sgu_b_s[j], sgu_w_out[j])
        x = layer_norm(DN_ALPHA * x + m, ln_g[i, 1], ln_b[i, 1])
        x = layer_norm(DN_ALPHA * x + 0.5 * swiglu(x, ffn_w_gate[i, 1], ffn_w_up[i, 1], ffn_w_down[i, 1]),
                       ln_g[i, 2], ln_b[i, 2])
        x = x + jax.nn.sigmoid(x @ ple_w_gate[i]) * (p[i] @ ple_w_proj[i])
    return x


_drawn_inputs = setup_inputs


def setup_inputs(seed=0):
    import zlib

    import numpy as np

    out = dict(_drawn_inputs(seed))
    spreads = {}
    factors = {'rel_bias': 3.184, 'sgu_b_in': 8.0, 'sgu_ln_g': 8.0, 'sgu_ln_b': 8.0, 'sgu_b_s': 2.843}
    for name, (base, spread) in spreads.items():
        noise = np.random.default_rng([zlib.crc32(name.encode()), seed]).standard_normal(out[name].shape)
        drawn = base * np.exp(spread * noise) if base else spread * noise
        out[name] = __import__('jax').numpy.asarray(drawn.astype(out[name].dtype))
    for name, factor in factors.items():
        out[name] = (out[name] * factor).astype(out[name].dtype)
    return out
```

```python
import math
from contextlib import ExitStack

import numpy as np

import concourse.bass as bass
from concourse import mybir

F32 = mybir.dt.float32
F32R = mybir.dt.float32r
ALU = mybir.AluOpType
ACT = mybir.ActivationFunctionType
AXX = mybir.AxisListType.X

P = 128
D = 1024
S = 256
HALVES = S // P
KB = D // P
FF = 2816
FC = 256
NCH = FF // FC
HD = 64
HEADS = 8
PLE = 256
DEPTH = 2
ALPHA = (2.0 * DEPTH) ** 0.25
EPS = 1e-5
NEG = -1e30
SCALE = HD ** -0.5
BUCKETS = 32
PHASES = [("ffn", 0, 0), ("attn", 0, 1), ("ffn", 0, 2), ("ple", 0, 0),
          ("ffn", 1, 0), ("sgu", 1, 1), ("ffn", 1, 2), ("ple", 1, 0)]
SGU_ORDER = [2, 3, 0, 1]


def phase_bases():
    per = {"ffn": dict(g=NCH, d=NCH, u=NCH, t=NCH + 2, v=NCH + 2, a=2 * NCH, x=4, r=4, ln=1),
           "attn": dict(g=8, d=0, u=6, t=5 + HEADS + 2 + 2, v=4, a=0, x=8, r=4, ln=1),
           "sgu": dict(g=6, d=0, u=4, t=1 + 2 + 2, v=4, a=8, x=8, r=4, ln=2),
           "ple": dict(g=2, d=1, u=2, t=1 + 2, v=1 + 2, a=4, x=4, r=0, ln=0)}
    now = dict(g=0, d=0, u=0, t=2, v=2, a=0, x=0, r=0, ln=0)
    out = []
    for kind, _, _ in PHASES:
        out.append(dict(now))
        now = {k: now[k] + per[kind][k] for k in now}
    return out, now


def build(nc, bucket_onehot, x_in, p_in, ln_g, ln_b, w_gate, w_up, w_down, attn_w_in, attn_b_f, attn_w_out,
          rel_bias, sgu_w_in, sgu_b_in, sgu_ln_g, sgu_ln_b, sgu_w_s, sgu_b_s, sgu_w_out, ple_w_proj,
          ple_w_gate, out):
    bases, total = phase_bases()
    bias_rows = nc.dram_tensor("bias_rows", (HEADS, 512), F32, kind="Internal").ap()

    with ExitStack() as ctx:
        def sb(name, shape, dt=F32, where=ctx):
            return where.enter_context(nc.sbuf_tensor(name, shape, dt))

        def sem(name):
            return ctx.enter_context(nc.semaphore(name))

        rawA = sb("rawA", [P, 4, 512])
        rawB = sb("rawB", [P, 4, 512])
        rawD = sb("rawD", [P, 2, D])
        g_hi = sb("g_hi", [P, 2, KB, 512], F32R)
        g_lo = sb("g_lo", [P, 2, KB, 512], F32R)
        x_tok = sb("x_tok", [P, HALVES, D])
        t_tok = sb("t_tok", [P, HALVES, D])
        xT_hi = sb("xT_hi", [P, KB, S], F32R)
        xT_lo = sb("xT_lo", [P, KB, S], F32R)
        stage = sb("stage", [P, HALVES, 512])
        hT_hi = sb("hT_hi", [P, HALVES, 2, P], F32R)
        hT_lo = sb("hT_lo", [P, HALVES, 2, P], F32R)
        gamma = sb("gamma", [P, D])
        beta = sb("beta", [P, D])
        bias_tab = sb("bias_tab", [P, 2048])
        p_tok = sb("p_tok", [P, HALVES, PLE])
        probs = sb("probs", [P, 2, 384])
        logits = sb("logits", [P, 2, 384])
        probsT = sb("probsT", [P, 2, 384])
        ident = sb("ident", [P, P])
        flip = sb("flip", [P, P])
        wf_raw = sb("wf_raw", [P, KB, HEADS])
        wf_hi = sb("wf_hi", [P, KB, HEADS], F32R)
        wf_lo = sb("wf_lo", [P, KB, HEADS], F32R)
        small = sb("small", [P, 256])
        zf = small[:, 0:16].rearrange("p (h n) -> p h n", h=2)
        c_tok = small[:, 16:32].rearrange("p (h n) -> p h n", h=2)
        bf_row = small[:, 32:40]
        row_sum = small[:, 40:72].rearrange("p (i n) -> p i n", i=2)
        row_inv = small[:, 72:104].rearrange("p (i n) -> p i n", i=2)
        row_max = small[:, 104:108].rearrange("p (b i) -> p b i", b=2)
        neg_max = small[:, 108:112].rearrange("p (b i) -> p b i", b=2)
        stats = small[:, 112:136].rearrange("p (h n) -> p h n", h=2)
        mean_var = small[:, 136:140].rearrange("p (h n) -> p h n", h=2)
        var_eps = small[:, 140:142]
        rstd = small[:, 142:144]
        neg_half = small[:, 144:145]
        bs_col = small[:, 152:160]
        with ExitStack() as region:
            d_hi = sb("d_hi", [P, 2, 2, D], F32R, region)
            d_lo = sb("d_lo", [P, 2, 2, D], F32R, region)
        with ExitStack() as region:
            qT = sb("qT", [P, HEADS, S], where=region)
            kT = sb("kT", [P, HEADS, S], where=region)
            v_att = sb("v_att", [P, HALVES, 2 * 512], where=region)
            head_c = sb("head_c", [HEADS, 2048], where=region)
        bias_rev = v_att
        with ExitStack() as region:
            u_sgu = sb("u_sgu", [P, HALVES, D], where=region)
            v_sgu = sb("v_sgu", [P, HALVES, D], where=region)
            ws_tok = sb("ws_tok", [P, HEADS, P], where=region)
            ws_T = sb("ws_T", [P, HEADS, P], where=region)
        region_end = sb("region_tail", [P, 2, 2 * D + 2 * D])
        del region_end
        causal = sb("causal", [P, S])
        causal_c = sb("causal_c", [P, 2, 384])
        sel = sb("sel", [HEADS, HEADS * P])
        rel_sb = sb("rel_sb", [BUCKETS, HEADS])
        onehot_sb = probs[0:BUCKETS, :, :].rearrange("p a b -> p (a b)")[:, 0:512]
        bias_row_sb = logits[0:HEADS, :, :].rearrange("p a b -> p (a b)")[:, 0:512]
        lf = head_c[:, :].rearrange("p (n s) -> p n s", s=S)

        acc = [ctx.enter_context(nc.psum_tensor(f"acc{h}", [P, 2, 512], F32)) for h in range(2)]
        gu = [ctx.enter_context(nc.psum_tensor(f"gu{h}", [P, 512], F32)) for h in range(2)]
        tp = [ctx.enter_context(nc.psum_tensor(f"tp{h}", [P, 512], F32)) for h in range(2)]

        raw_a, raw_b, raw_d = sem("raw_a"), sem("raw_b"), sem("raw_d")
        high_a, high_b, high_d = sem("high_a"), sem("high_b"), sem("high_d")
        split_a, split_b, split_d = sem("split_a"), sem("split_b"), sem("split_d")
        g_done = sem("g_done")
        d_done = sem("d_done")
        gu_taken = [sem("gu_taken0"), sem("gu_taken1")]
        tp_full = [sem("tp_full0"), sem("tp_full1")]
        tp_hi = [sem("tp_hi0"), sem("tp_hi1")]
        tp_taken = [sem("tp_taken0"), sem("tp_taken1")]
        act_done = sem("act_done")
        tok_ready = sem("tok_ready")
        acc_read = sem("acc_read")
        x_loaded, p_loaded = [sem("x_loaded0"), sem("x_loaded1")], sem("p_loaded")
        ln_loaded = sem("ln_loaded")
        var_ready, rstd_ready = sem("var_ready"), sem("rstd_ready")
        step = sem("step")
        const_ready, pool_step = sem("const_ready"), sem("pool_step")
        bias_in, bias_mm, bias_sb, bias_st, bias_ld, bias_flip, bias_done = (
            sem("bias_in"), sem("bias_mm"), sem("bias_sb"), sem("bias_st"), sem("bias_ld"), sem("bias_flip"),
            sem("bias_done"))
        f_loaded, f_hi, f_split, f_mm, f_tok, f_exp, f_arg, f_ln, f_cum = (
            sem("f_loaded"), sem("f_hi"), sem("f_split"), sem("f_mm"), sem("f_tok"), sem("f_exp"),
            sem("f_arg"), sem("f_ln"), sem("f_cum"))
        s_full, s_taken, p_ready, pv_done = sem("s_full"), sem("s_taken"), sem("p_ready"), sem("pv_done")
        ws_loaded, vn_ready, mix_done, sgu_bias_ld, ws_raw = (
            sem("ws_loaded"), sem("vn_ready"), sem("mix_done"), sem("sgu_bias_ld"),
            sem("ws_raw"))
        rows_loaded = sem("rows_loaded")
        out_done = sem("out_done")

        block = ctx.enter_context(nc.Block())

        def g_source(k, c, part):
            kind, i, s = PHASES[k]
            rows = slice(4 * part, 4 * part + 4)
            if kind == "ffn":
                cols = bass.DynSlice(c * FC, FC)
                gate = w_gate[i, s // 2].rearrange("(b p) n -> p b n", p=P)[:, rows, cols]
                up = w_up[i, s // 2].rearrange("(b p) n -> p b n", p=P)[:, rows, cols]
                return [(slice(0, 4), slice(0, FC), gate), (slice(0, 4), slice(FC, 2 * FC), up)]
            if kind == "attn":
                w, c = (attn_w_in[0], c) if c < 6 else (attn_w_out[0], c - 6)
            elif kind == "sgu":
                w, c = (sgu_w_in[0], SGU_ORDER[c]) if c < 4 else (sgu_w_out[0], c - 4)
            else:
                w = ple_w_gate[i]
            v = w.rearrange("(b p) n -> p b n", p=P)[:, rows, 512 * c:512 * c + 512]
            return [(slice(0, 2), slice(0, 512), v[:, 0:2]), (slice(2, 4), slice(0, 512), v[:, 2:4])]

        @block.sync
        def _(sp):
            def load_g(n, k, c):
                for part, raw, loaded, split in ((0, rawA, raw_a, split_a), (1, rawB, raw_b, split_b)):
                    if not (isinstance(n, int) and n == 0):
                        sp.wait_ge(split, n)
                    for b, cols, src in g_source(k, c, part):
                        sp.dma_start(raw[:, b, cols], src).then_inc(loaded, 16)

            def load_d(m, src):
                if not (isinstance(m, int) and m == 0):
                    sp.wait_ge(split_d, m)
                sp.dma_start(rawD[:, :, :], src).then_inc(raw_d, 16)

            for h in range(HALVES):
                sp.dma_start(x_tok[:, h, :], x_in[0, h * P:(h + 1) * P, :]).then_inc(x_loaded[h], 16)
            load_g(0, 0, 0)
            for k, (kind, i, s) in enumerate(PHASES):
                g0, d0 = bases[k]["g"], bases[k]["d"]
                chunks = {"ffn": NCH, "attn": 8, "sgu": 6, "ple": 2}[kind]

                def load_next(c):
                    if c + 1 < chunks:
                        load_g(g0 + c + 1, k, c + 1)
                    elif k + 1 < len(PHASES):
                        load_g(g0 + c + 1, k + 1, 0)

                if kind == "ffn":
                    down = w_down[i, s // 2].rearrange("(c b p) n -> p c b n", b=2, p=P)
                    load_next(0)
                    load_d(d0, down[:, 0])
                    with sp.Fori(1, NCH - 1) as c:
                        load_g(g0 + 1 + c, k, c + 1)
                        load_d(d0 + c, down[:, bass.DynSlice(c, 1)])
                    load_next(NCH - 1)
                    load_d(d0 + NCH - 1, down[:, NCH - 1])
                    if s == 2:
                        load_d(d0 + NCH, ple_w_proj[i].rearrange("(b p) n -> p b n", p=P))
                else:
                    for c in range(chunks):
                        load_next(c)
            for n, (j, h) in enumerate([(j, h) for j in range(2) for h in range(2)]):
                sp.wait_ge(tok_ready, bases[-1]["x"] + n + 1)
                sp.dma_start(out[0, h * P:(h + 1) * P, 512 * j:512 * j + 512],
                             x_tok[:, h, 512 * j:512 * j + 512]).then_inc(out_done, 16)
            sp.wait_ge(out_done, 4 * 16)

        @block.tensor
        def _(pe):
            def product(dst, hi, lo, w_hi, w_lo, first=True, last=True):
                for b in range(len(hi)):
                    pe.matmul(dst, hi[b], w_hi[b], start=first and b == 0, stop=False)
                    pe.matmul(dst, hi[b], w_lo[b], start=False, stop=False)
                    done = pe.matmul(dst, lo[b], w_hi[b], start=False, stop=last and b == len(hi) - 1)
                return done

            def g_product(n, slot, h, dst, free=None):
                if free is not None:
                    pe.wait_ge(gu_taken[h], free)
                tok = slice(h * P, (h + 1) * P)
                for part, split in ((0, split_a), (1, split_b)):
                    if h == 0:
                        pe.wait_ge(split, n + 1)
                    ks = range(4 * part, 4 * part + 4)
                    done = product(dst, [xT_hi[:, b, tok] for b in ks], [xT_lo[:, b, tok] for b in ks],
                                   [g_hi[:, slot, b, :] for b in ks], [g_lo[:, slot, b, :] for b in ks],
                                   first=part == 0, last=part == 1)
                done.then_inc(g_done, 1)

            def d_product(m, slot, h, first, last):
                pe.wait_ge(split_d, m + 1)
                for j in range(2):
                    cols = slice(512 * j, 512 * j + 512)
                    done = product(acc[h][:, j, :], [hT_hi[:, h, b, :] for b in range(2)],
                                   [hT_lo[:, h, b, :] for b in range(2)],
                                   [d_hi[:, slot, b, cols] for b in range(2)],
                                   [d_lo[:, slot, b, cols] for b in range(2)], first=first, last=last)
                done.then_inc(d_done, 1)

            def transposes(bank, use, srcs, width=P):
                if not (isinstance(use, int) and use == 0):
                    pe.wait_ge(tp_taken[bank], use)
                for q, src in enumerate(srcs):
                    rows = src.shape[0]
                    done = pe.transpose(tp[bank][0:src.shape[1], rows * q:rows * q + rows], src,
                                        ident[0:rows, 0:rows])
                done.then_inc(tp_full[bank], 1)

            def token_transposes(src, h, use, needs):
                for j in range(2):
                    pe.wait_ge(*needs[j])
                    transposes(j, use, [src[:, h, 512 * j + P * q:512 * j + P * q + P] for q in range(4)])

            def xT_wait(h, use):
                for j in range(2):
                    pe.wait_ge(tp_taken[j], use + h + 1)

            pe.wait_ge(const_ready, 1)
            use = 0
            for h in range(HALVES):
                token_transposes(x_tok, h, h, [(x_loaded[h], 16)] * 2)

            pending = None
            for k, (kind, i, s) in enumerate(PHASES):
                B = bases[k]
                g0, d0, u0, t0, x0 = B["g"], B["d"], B["u"], B["t"], B["x"]

                def ln_transposes(tok0, at):
                    for h in range(HALVES):
                        token_transposes(x_tok, h, at + h, [(tok_ready, tok0 + 2 * h + j + 1) for j in range(2)])
                        yield

                if kind == "ffn":
                    def up(c, cs, h):
                        free = u0 + c
                        g_product(g0 + c, (g0 + cs) % 2, h, gu[h][:, :],
                                  None if isinstance(free, int) and free == 0 else free)

                    def turn(c, h):
                        pe.wait_ge(gu_taken[h], u0 + c + 1)
                        transposes(h, t0 + c, [stage[:, h, FC + P * b:FC + P * b + P] for b in range(2)])

                    def down(c, cs, h):
                        pe.wait_ge(tp_taken[h], t0 + c + 1)
                        d_product(d0 + c, (d0 + cs) % 2, h, first=cs == 0, last=cs == NCH - 1)

                    def chunk(c, cs):
                        up(c, cs, 0)
                        turn(c - 1, 1)
                        down(c - 1, cs - 1, 0)
                        up(c, cs, 1)
                        turn(c, 0)
                        down(c - 1, cs - 1, 1)

                    xT_wait(0, use)
                    up(0, 0, 0)
                    if pending is not None:
                        next(pending)
                    xT_wait(1, use)
                    up(0, 0, 1)
                    if k == 0:
                        pe.wait_ge(bias_in, 32)
                        pe.matmul(acc[1][0:HEADS, 1, :], rel_sb[:, :], onehot_sb, start=True,
                                  stop=True).then_inc(bias_mm, 1)
                    turn(0, 0)
                    if k == 0:
                        pe.wait_ge(bias_sb, 1)
                    chunk(1, 1)
                    chunk(2, 2)
                    with pe.Fori(0, (NCH - 3) // 2) as r:
                        for e in range(2):
                            chunk(r * 2 + (3 + e), 3 + e)
                    turn(NCH - 1, 1)
                    down(NCH - 1, NCH - 1, 0)
                    down(NCH - 1, NCH - 1, 1)
                    use = t0 + NCH
                    pending = ln_transposes(x0, use)
                    if s != 2:
                        next(pending)
                    continue

                if kind == "ple":
                    next(pending)
                    xT_wait(0, use)
                    g_product(g0, g0 % 2, 0, gu[0][:, :], u0)
                    next(pending)
                    pe.wait_ge(p_loaded, 16 * (i + 1))
                    for h in range(HALVES):
                        transposes(h, t0, [p_tok[:, h, P * b:P * b + P] for b in range(2)])
                    xT_wait(1, use)
                    g_product(g0, g0 % 2, 1, gu[1][:, :], u0)
                    for h in range(HALVES):
                        pe.wait_ge(tp_taken[h], t0 + 1)
                        d_product(d0, d0 % 2, h, first=True, last=True)
                    for h in range(HALVES):
                        g_product(g0 + 1, (g0 + 1) % 2, h, gu[h][:, :], u0 + 1)
                    if k + 1 < len(PHASES):
                        use = t0 + 1

                        def ple_transposes(tok0, at):
                            for h in range(HALVES):
                                token_transposes(x_tok, h, at + h, [(tok_ready, tok0 + 3 + h)] * 2)
                                yield
                        pending = ple_transposes(x0, use)
                        next(pending)
                    continue

                if kind == "attn":
                    xT_wait(0, use)
                    tp_use = [t0, t0]

                    def qk_turn(c, h):
                        pe.wait_ge(gu_taken[h], u0 + c + 1)
                        transposes(h, tp_use[h], [stage[:, h, P * q:P * q + P] for q in range(4)])
                        tp_use[h] += 1

                    for c in range(6):
                        g_product(g0 + c, (g0 + c) % 2, 0, gu[0][:, :], u0 + c)
                        if c == 0:
                            next(pending)
                            xT_wait(1, use)
                        elif c % 3 != 0:
                            qk_turn(c - 1, 1)
                        if c == 1:
                            pe.wait_ge(f_tok, 2)
                            transposes(0, tp_use[0], [zf[:, h, :] for h in range(2)])
                            tp_use[0] += 1
                            pe.wait_ge(bias_ld, 16)
                            for q in range(4):
                                done = pe.matmul(acc[q // 2][:, q % 2, :], flip[:, :],
                                                 bias_rev[:, q // 2, 512 * (q % 2):512 * (q % 2) + 512],
                                                 start=True, stop=True)
                            done.then_inc(bias_flip, 1)
                        if c == 2:
                            pe.wait_ge(f_cum, 1)
                            pe.wait_ge(tp_taken[1], tp_use[1])
                            for h in range(2):
                                done = pe.transpose(tp[1][:, HEADS * h:HEADS * h + HEADS],
                                                    lf[:, 0, h * P:(h + 1) * P], ident[0:HEADS, 0:HEADS])
                            done.then_inc(tp_full[1], 1)
                            tp_use[1] += 1
                        g_product(g0 + c, (g0 + c) % 2, 1, gu[1][:, :], u0 + c)
                        if c % 3 != 2:
                            qk_turn(c, 0)
                        if c == 0:
                            pe.wait_ge(f_split, 1)
                            for h in range(HALVES):
                                tok = slice(h * P, (h + 1) * P)
                                done = product(acc[h][:, 0, 0:HEADS], [xT_hi[:, b, tok] for b in range(KB)],
                                               [xT_lo[:, b, tok] for b in range(KB)],
                                               [wf_hi[:, b, :] for b in range(KB)],
                                               [wf_lo[:, b, :] for b in range(KB)])
                                done.then_inc(f_mm, 1)

                    def scores(n):
                        g, hh, sl = n // HEADS, n % HEADS, n % 2
                        rows, blk = slice(HD * (hh % 2), HD * (hh % 2) + HD), 4 * g + hh // 2
                        if n == 0:
                            pe.wait_ge(bias_done, 1)
                            for b in range(2):
                                pe.wait_ge(tp_taken[b], tp_use[b])
                        if n >= 2:
                            pe.wait_ge(s_taken, n - 1)
                        for i_q, cols in ((1, slice(0, S)), (0, slice(S, S + P))):
                            wide = cols.stop - cols.start
                            dst = acc[0][:, sl, cols]
                            done = pe.matmul(dst, qT[rows, blk, i_q * P:i_q * P + P], kT[rows, blk, 0:wide],
                                             start=True, stop=g == 0)
                            if g == 1:
                                done = pe.matmul(dst, sel[:, hh * P:hh * P + P], lf[:, 1, 0:wide],
                                                 start=False, stop=True)
                        done.then_inc(s_full, 1)

                    def probs_turn(n):
                        pe.wait_ge(p_ready, n + 1)
                        b = n % 2
                        transposes(b, tp_use[b], [probs[:, b, P * q:P * q + P] for q in range(3)])
                        tp_use[b] += 1

                    def values(n):
                        g, hh, sl = n // HEADS, n % HEADS, n % 2
                        pe.wait_ge(tp_taken[sl], t0 + 5 + n // 2 + 1)
                        if n == 0:
                            for h in range(HALVES):
                                pe.wait_ge(gu_taken[h], u0 + 6)
                        if n == HEADS:
                            pe.wait_ge(tok_ready, x0 + 2)
                        vc = slice(g * 512 + hh * HD, g * 512 + hh * HD + HD)
                        oc = slice(hh * HD, hh * HD + HD)
                        pe.matmul(acc[1][:, 0, oc], probsT[:, sl, 2 * P:3 * P], v_att[:, 0, vc],
                                  start=True, stop=True)
                        pe.matmul(acc[1][:, 1, oc], probsT[:, sl, 0:P], v_att[:, 0, vc], start=True, stop=False)
                        pe.matmul(acc[1][:, 1, oc], probsT[:, sl, P:2 * P], v_att[:, 1, vc],
                                  start=False, stop=True).then_inc(pv_done, 1)

                    for n in range(2 * HEADS + 2):
                        if n < 2 * HEADS:
                            scores(n)
                        if 1 <= n <= 2 * HEADS:
                            probs_turn(n - 1)
                        if n >= 2:
                            values(n - 2)
                    use = t0 + 5 + HEADS
                    for h in range(HALVES):
                        token_transposes(t_tok, h, use + h, [(tok_ready, x0 + 2 + h + 1)] * 2)
                    out_chunks, out0 = 6, g0 + 6

                if kind == "sgu":
                    xT_wait(0, use)
                    for c in range(4):
                        g_product(g0 + c, (g0 + c) % 2, 0, gu[0][:, :], u0 + c)
                        if c == 0:
                            next(pending)
                            xT_wait(1, use)
                        g_product(g0 + c, (g0 + c) % 2, 1, gu[1][:, :], u0 + c)
                        if c == 0:
                            pe.wait_ge(ws_loaded, 1)
                            for b in range(2):
                                transposes(b, t0, [ws_tok[:, 4 * b + q, :] for q in range(4)])
                    for h in range(HALVES):
                        if h == 0:
                            for b in range(2):
                                pe.wait_ge(tp_taken[b], t0 + 1)
                        pe.wait_ge(vn_ready, 2 * (h + 1))
                        for g in range(HEADS):
                            done = pe.matmul(acc[h][:, g // 4, P * (g % 4):P * (g % 4) + P], ws_T[:, g, :],
                                             v_sgu[:, h, P * g:P * g + P], start=True, stop=True)
                        done.then_inc(mix_done, 1)
                    use = t0 + 1
                    for h in range(HALVES):
                        token_transposes(t_tok, h, use + h, [(tok_ready, x0 + 2 * h + j + 1) for j in range(2)])
                    out0 = g0 + 4

                for j in range(2):
                    for h in range(HALVES):
                        if j == 0:
                            xT_wait(h, use)
                        g_product(out0 + j, (out0 + j) % 2, h, acc[h][:, j, :])
                use += 2
                pending = ln_transposes(x0 + 4, use)
                next(pending)

        @block.scalar
        def _(act):
            def copy(dst, src, scale=1.0):
                return act.activation(dst, src, ACT.Copy, scale=scale)

            def hi_g(n, slot, part):
                raw, loaded, done = ((rawA, raw_a, high_a), (rawB, raw_b, high_b))[part]
                act.wait_ge(loaded, 32 * n + 32)
                if not (isinstance(n, int) and n < 2):
                    act.wait_ge(g_done, 2 * n - 2)
                copy(g_hi[:, slot, 4 * part:4 * part + 4, :], raw[:, :, :]).then_inc(done, 1)

            def hi_d(m, slot):
                act.wait_ge(raw_d, 16 * m + 16)
                if not (isinstance(m, int) and m < 2):
                    act.wait_ge(d_done, 2 * m - 2)
                copy(d_hi[:, slot, :, :], rawD[:, :, :]).then_inc(high_d, 1)

            def xT_high(h, use):
                for j in range(2):
                    act.wait_ge(tp_full[j], use + h + 1)
                    copy(xT_hi[:, 4 * j:4 * j + 4, h * P:(h + 1) * P],
                         tp[j][:, :].rearrange("p (b t) -> p b t", b=4)).then_inc(tp_hi[j], 1)

            def hT_high(h, use):
                act.wait_ge(tp_full[h], use + 1)
                copy(hT_hi[:, h, :, :], tp[h][:, 0:2 * P].rearrange("p (b t) -> p b t", b=2)).then_inc(tp_hi[h], 1)

            for h in range(HALVES):
                xT_high(h, 0)
            hi_g(0, 0, 0)
            hi_g(0, 0, 1)
            for k, (kind, i, s) in enumerate(PHASES):
                B = bases[k]
                g0, d0, u0, t0, a0 = B["g"], B["d"], B["u"], B["t"], B["a"]
                last_phase = k + 1 == len(PHASES)

                if kind == "ffn":
                    def gate(c, h):
                        act.wait_ge(g_done, 2 * c + (2 * g0 + h + 1))
                        act.activation(stage[:, h, 0:FC], gu[h][:, 0:FC], ACT.Silu).then_inc(act_done, 1)

                    def chunk(c, cs):
                        slot = (g0 + cs + 1) % 2
                        hi_g(c + (g0 + 1), slot, 0)
                        gate(c, 0)
                        if cs > 0:
                            hT_high(1, c + (t0 - 1))
                        hi_g(c + (g0 + 1), slot, 1)
                        gate(c, 1)
                        hT_high(0, c + t0)
                        hi_d(c + d0, (d0 + cs) % 2)

                    for c in range(3):
                        chunk(c, c)
                    with act.Fori(0, (NCH - 3) // 2) as r:
                        for e in range(2):
                            chunk(r * 2 + (3 + e), 3 + e)
                    hT_high(1, t0 + NCH - 1)
                    if s == 2:
                        hi_d(d0 + NCH, (d0 + NCH) % 2)
                    if s == 0:
                        if i == 0:
                            act.wait_ge(f_loaded, 16)
                            copy(wf_hi[:, :, :], wf_raw[:, :, :]).then_inc(f_hi, 1)
                    for h in range(HALVES):
                        xT_high(h, t0 + NCH)

                if kind == "ple":
                    for j in range(2):
                        for h in range(HALVES):
                            if not (last_phase and j == 1):
                                hi_g(g0 + j + 1, (g0 + j + 1) % 2, h)
                            if j == 0:
                                hT_high(h, t0)
                            act.wait_ge(g_done, 2 * (g0 + j) + h + 1)
                            if j == 1:
                                act.wait_ge(tok_ready, B["x"] + h + 1)
                            act.activation(stage[:, h, :], gu[h][:, :], ACT.Sigmoid).then_inc(act_done, 1)
                    if not last_phase:
                        for h in range(HALVES):
                            xT_high(h, t0 + 1)

                if kind == "attn":
                    tq = t0
                    for c in range(6):
                        for h in range(HALVES):
                            hi_g(g0 + c + 1, (g0 + c + 1) % 2, h)
                            act.wait_ge(g_done, 2 * (g0 + c) + h + 1)
                            if c % 3 == 2:
                                g = c // 3
                                copy(v_att[:, h, 512 * g:512 * g + 512], gu[h][:, :]).then_inc(gu_taken[h], 1)
                            else:
                                if c > 0:
                                    n_before = {(0, 1): 1, (0, 3): 3, (0, 4): 4, (1, 1): 1, (1, 3): 2, (1, 4): 4}
                                    act.wait_ge(tp_full[h], t0 + n_before[(h, c)])
                                copy(stage[:, h, :], gu[h][:, :], SCALE if c % 3 == 0 else 1.0)\
                                    .then_inc(gu_taken[h], 1)
                        if c == 1:
                            act.wait_ge(f_arg, 1)
                            act.activation(lf[:, 3, :], lf[:, 2, :], ACT.Exp).then_inc(f_exp, 1)
                            act.wait_ge(f_arg, 2)
                            act.activation(lf[:, 5, :], lf[:, 4, :], ACT.Ln).then_inc(f_ln, 1)

                    for part in range(2):
                        hi_g(g0 + 7, (g0 + 7) % 2, part)

                    def probs_copy(n):
                        b = n % 2
                        act.wait_ge(tp_full[b], t0 + 5 + n // 2 + 1)
                        if n >= 2:
                            act.wait_ge(pv_done, n - 1)
                        copy(probsT[:, b, :], tp[b][:, 0:384]).then_inc(tp_taken[b], 1)

                    for n in range(2 * HEADS + 1):
                        if n < 2 * HEADS:
                            b = n % 2
                            act.wait_ge(s_taken, n + 1)
                            for q, cols in ((0, slice(0, S)), (1, slice(S, S + P))):
                                done = act.activation(probs[:, b, cols], logits[:, b, cols], ACT.Exp,
                                                      bias=neg_max[:, b, q:q + 1],
                                                      accum_out=row_sum[:, 1 - q, n:n + 1])
                            done.then_inc(p_ready, 1)
                        if n >= 1:
                            probs_copy(n - 1)
                    for h in range(HALVES):
                        xT_high(h, t0 + 5 + HEADS)
                    for part in range(2):
                        hi_g(g0 + 8, (g0 + 8) % 2, part)
                    for h in range(HALVES):
                        xT_high(h, t0 + 5 + HEADS + 2)

                if kind == "sgu":
                    for c in range(4):
                        dst = (v_sgu, u_sgu)[c // 2]
                        for h in range(HALVES):
                            hi_g(g0 + c + 1, (g0 + c + 1) % 2, h)
                            act.wait_ge(gu_taken[h], u0 + c + 1)
                            act.activation(dst[:, h, 512 * (c % 2):512 * (c % 2) + 512], stage[:, h, :],
                                           ACT.Gelu_apprx_tanh).then_inc(act_done, 1)
                        if c == 0:
                            for b in range(2):
                                act.wait_ge(tp_full[b], t0 + 1)
                                copy(ws_T[:, 4 * b:4 * b + 4, :],
                                     tp[b][:, :].rearrange("p (b t) -> p b t", b=4)).then_inc(tp_taken[b], 1)
                    for h in range(HALVES):
                        xT_high(h, t0 + 1)
                    for j in range(2):
                        hi_g(g0 + 5 + j, (g0 + 5 + j) % 2, 0)
                        hi_g(g0 + 5 + j, (g0 + 5 + j) % 2, 1)
                    for h in range(HALVES):
                        xT_high(h, t0 + 3)

        @block.vector
        def _(dve):
            steps = [0]

            def link(instruction):
                instruction.then_inc(step, 1)
                steps[0] += 1
                dve.wait_ge(step, steps[0])

            def low(dst, src, hi):
                return dve.tensor_tensor(dst, src, hi.bitcast(F32), ALU.subtract)

            def lo_g(n, slot, part):
                raw, high, done = ((rawA, high_a, split_a), (rawB, high_b, split_b))[part]
                ks = slice(4 * part, 4 * part + 4)
                dve.wait_ge(high, n + 1)
                low(g_lo[:, slot, ks, :], raw[:, :, :], g_hi[:, slot, ks, :]).then_inc(done, 1)

            def lo_d(m, slot):
                dve.wait_ge(high_d, m + 1)
                low(d_lo[:, slot, :, :], rawD[:, :, :], d_hi[:, slot, :, :]).then_inc(split_d, 1)

            def xT_low(h, use):
                for j in range(2):
                    dve.wait_ge(tp_hi[j], use + h + 1)
                    part = (slice(None), slice(4 * j, 4 * j + 4), slice(h * P, (h + 1) * P))
                    low(xT_lo[part], tp[j][:, :].rearrange("p (b t) -> p b t", b=4), xT_hi[part])\
                        .then_inc(tp_taken[j], 1)

            def hT_low(h, use):
                dve.wait_ge(tp_hi[h], use + 1)
                low(hT_lo[:, h, :, :], tp[h][:, 0:2 * P].rearrange("p (b t) -> p b t", b=2), hT_hi[:, h, :, :])\
                    .then_inc(tp_taken[h], 1)

            def normalise(src, dst, h, ln, ready):
                for j in range(2):
                    link(dve.bn_stats(stats[:, h, 6 * j:6 * j + 6], src[:, 512 * j:512 * j + 512]))
                link(dve.bn_aggr(mean_var[:, h, :], stats[:, h, :]))
                dve.tensor_scalar(var_eps[:, h:h + 1], mean_var[:, h, 1:2], EPS, None, ALU.add)\
                    .then_inc(var_ready, 1)
                dve.wait_ge(rstd_ready, 2 * ln + h + 1)
                if h == 0:
                    dve.wait_ge(ln_loaded, 32 * (ln + 1))
                for j in range(2):
                    cols = slice(512 * j, 512 * j + 512)
                    link(dve.tensor_scalar(src[:, cols], src[:, cols], mean_var[:, h, 0:1], rstd[:, h:h + 1],
                                           ALU.subtract, ALU.mult))
                    link(dve.tensor_tensor(src[:, cols], src[:, cols], gamma[:, cols], ALU.mult))
                    dve.tensor_tensor(dst[:, cols], src[:, cols], beta[:, cols], ALU.add).then_inc(ready, 1)

            def residual_norm(h, ln, r0, needs):
                for j in range(2):
                    dve.wait_ge(*needs[j])
                    dve.scalar_tensor_tensor(out=t_tok[:, h, 512 * j:512 * j + 512],
                                             in0=x_tok[:, h, 512 * j:512 * j + 512], scalar=ALPHA,
                                             in1=acc[h][:, j, :], op0=ALU.mult, op1=ALU.add)\
                        .then_inc(acc_read, 1)
                dve.wait_ge(acc_read, r0 + 2 * h + 2)
                normalise(t_tok[:, h, :], x_tok[:, h, :], h, ln, tok_ready)

            for h in range(HALVES):
                xT_low(h, 0)
            lo_g(0, 0, 0)
            lo_g(0, 0, 1)
            for k, (kind, i, s) in enumerate(PHASES):
                B = bases[k]
                g0, d0, u0, t0, v0, a0, x0, r0, ln0 = (B[q] for q in ("g", "d", "u", "t", "v", "a", "x", "r", "ln"))
                last_phase = k + 1 == len(PHASES)

                if kind == "ffn":
                    def gated(c, h):
                        dve.wait_ge(act_done, 2 * c + (a0 + h + 1))
                        dve.scalar_tensor_tensor(out=stage[:, h, FC:2 * FC], in0=stage[:, h, 0:FC], scalar=0.5,
                                                 in1=gu[h][:, FC:2 * FC], op0=ALU.mult, op1=ALU.mult)\
                            .then_inc(gu_taken[h], 1)

                    def chunk(c, cs):
                        slot = (g0 + cs + 1) % 2
                        lo_g(c + (g0 + 1), slot, 0)
                        gated(c, 0)
                        if cs > 0:
                            hT_low(1, c + (v0 - 1))
                        lo_g(c + (g0 + 1), slot, 1)
                        gated(c, 1)
                        hT_low(0, c + v0)
                        lo_d(c + d0, (d0 + cs) % 2)

                    chunk(0, 0)
                    if k == 0:
                        dve.wait_ge(bias_mm, 1)
                        link(dve.tensor_copy(bias_row_sb, acc[1][0:HEADS, 1, :]))
                        dve.memset(bias_row_sb[:, S:512], NEG).then_inc(bias_sb, 1)
                    chunk(1, 1)
                    chunk(2, 2)
                    with dve.Fori(0, (NCH - 3) // 2) as r:
                        for e in range(2):
                            chunk(r * 2 + (3 + e), 3 + e)
                    hT_low(1, v0 + NCH - 1)
                    if s == 2:
                        lo_d(d0 + NCH, (d0 + NCH) % 2)
                    for h in range(HALVES):
                        residual_norm(h, ln0, r0, [(d_done, 2 * (d0 + NCH - 1) + h + 1)] * 2)
                        xT_low(h, v0 + NCH)
                    if k == 0:
                        dve.wait_ge(f_hi, 1)
                        low(wf_lo[:, :, :], wf_raw[:, :, :], wf_hi[:, :, :]).then_inc(f_split, 1)

                if kind == "ple":
                    for j in range(2):
                        cols = slice(512 * j, 512 * j + 512)
                        for h in range(HALVES):
                            if not (last_phase and j == 1):
                                lo_g(g0 + j + 1, (g0 + j + 1) % 2, h)
                            if j == 0:
                                hT_low(h, v0)
                                dve.wait_ge(d_done, 2 * d0 + h + 1)
                            dve.wait_ge(act_done, a0 + 2 * j + h + 1)
                            dve.tensor_tensor(stage[:, h, :], stage[:, h, :], acc[h][:, j, :], ALU.mult)\
                                .then_inc(gu_taken[h], 1)
                            dve.wait_ge(gu_taken[h], u0 + j + 1)
                            dve.tensor_tensor(x_tok[:, h, cols], x_tok[:, h, cols], stage[:, h, :], ALU.add)\
                                .then_inc(tok_ready, 1)
                    if not last_phase:
                        for h in range(HALVES):
                            xT_low(h, v0 + 1)

                if kind == "attn":
                    tp_use = [t0, t0]

                    def qk_copy(c, h):
                        dst, g = (qT, kT)[c % 3], c // 3
                        dve.wait_ge(tp_full[h], tp_use[h] + 1)
                        tp_use[h] += 1
                        dve.tensor_copy(dst[:, 4 * g:4 * g + 4, h * P:(h + 1) * P],
                                        tp[h][:, :].rearrange("p (b t) -> p b t", b=4)).then_inc(tp_taken[h], 1)

                    for c in range(6):
                        lo_g(g0 + c + 1, (g0 + c + 1) % 2, 0)
                        if c % 3 != 0:
                            qk_copy(c - 1, 1)
                        if c == 1:
                            dve.wait_ge(tp_full[0], tp_use[0] + 1)
                            tp_use[0] += 1
                            dve.tensor_copy(lf[:, 6, :], tp[0][0:HEADS, 0:S]).then_inc(tp_taken[0], 1)
                            dve.wait_ge(tp_taken[0], tp_use[0])
                            link(dve.tensor_scalar(lf[:, 7, :], lf[:, 6, :], -1.0, None, ALU.mult))
                            dve.tensor_tensor(lf[:, 2, :], lf[:, 6, :], lf[:, 7, :], ALU.min).then_inc(f_arg, 1)
                        if c == 2:
                            dve.wait_ge(bias_flip, 1)
                            for q in range(4):
                                done = dve.tensor_copy(bias_tab[:, 512 * q:512 * q + 512],
                                                       acc[q // 2][:, q % 2, :])
                            done.then_inc(bias_done, 1)
                            dve.wait_ge(tp_full[1], tp_use[1] + 1)
                            tp_use[1] += 1
                            dve.tensor_copy(c_tok[:, :, :], tp[1][:, 0:2 * HEADS]
                                            .rearrange("p (h n) -> p h n", h=2)).then_inc(tp_taken[1], 1)
                        lo_g(g0 + c + 1, (g0 + c + 1) % 2, 1)
                        if c == 0:
                            for h in range(HALVES):
                                dve.wait_ge(f_mm, h + 1)
                                if h == 0:
                                    dve.wait_ge(rows_loaded, 32)
                                dve.tensor_tensor(zf[:, h, :], acc[h][:, 0, 0:HEADS], bf_row, ALU.add)\
                                    .then_inc(f_tok, 1)
                        if c % 3 != 2:
                            qk_copy(c, 0)
                        if c == 1:
                            dve.wait_ge(f_exp, 1)
                            link(dve.tensor_scalar(lf[:, 4, :], lf[:, 3, :], 1.0, None, ALU.add))
                            dve.tensor_scalar(lf[:, 7, :], lf[:, 4, :], -1.0, None, ALU.add).then_inc(f_arg, 1)
                            dve.wait_ge(f_arg, 2)
                            link(dve.tensor_tensor(lf[:, 7, :], lf[:, 3, :], lf[:, 7, :], ALU.subtract))
                            link(dve.reciprocal(lf[:, 0, :], lf[:, 4, :]))
                            link(dve.tensor_tensor(lf[:, 7, :], lf[:, 7, :], lf[:, 0, :], ALU.mult))
                            dve.wait_ge(f_ln, 1)
                            link(dve.tensor_tensor(lf[:, 5, :], lf[:, 5, :], lf[:, 7, :], ALU.add))
                            link(dve.tensor_scalar(lf[:, 7, :], lf[:, 6, :], 0.0, None, ALU.min))
                            link(dve.tensor_tensor(lf[:, 7, :], lf[:, 7, :], lf[:, 5, :], ALU.subtract))
                            link(dve.memset(lf[:, 2, :], 1.0))
                            link(dve.tensor_tensor_scan(lf[:, 0, :], lf[:, 2, :], lf[:, 7, :], 0.0,
                                                        ALU.mult, ALU.add))
                            dve.tensor_scalar(lf[:, 1, :], lf[:, 0, :], -1.0, None, ALU.mult).then_inc(f_cum, 1)
                    for part in range(2):
                        lo_g(g0 + 7, (g0 + 7) % 2, part)

                    def group_out(g):
                        dve.wait_ge(pv_done, HEADS * (g + 1))
                        cols = slice(HEADS * g, HEADS * g + HEADS)
                        link(dve.reciprocal(row_inv[:, :, cols], row_sum[:, :, cols]))
                        for q in range(2):
                            dve.tensor_tensor(
                                t_tok[:, q, 512 * g:512 * g + 512].rearrange("p (n d) -> p n d", d=HD),
                                acc[1][:, q, :].rearrange("p (n d) -> p n d", d=HD),
                                row_inv[:, q, cols].unsqueeze(2).to_broadcast([P, HEADS, HD]),
                                ALU.mult).then_inc(tok_ready, 1)

                    for n in range(2 * HEADS):
                        g, hh, b = n // HEADS, n % HEADS, n % 2
                        if n == 0:
                            dve.wait_ge(bias_done, 1)
                        pieces = ((0, slice(0, S), 0), (1, slice(S, S + P), P))
                        if g == 1:
                            for q, cols, at in pieces:
                                done = dve.tensor_scalar(causal_c[:, b, cols], causal[:, at:S],
                                                         c_tok[:, 1 - q, hh:hh + 1], None, ALU.add)
                            link(done)
                        dve.wait_ge(s_full, n + 1)
                        if n >= 2:
                            dve.wait_ge(p_ready, n - 1)
                        for q, cols, at in pieces:
                            add = (causal_c[:, b, cols] if g == 1
                                   else bias_tab[:, S * hh + at:S * hh + S])
                            done = dve.tensor_tensor_reduce(
                                out=logits[:, b, cols], in0=acc[0][:, b, cols], in1=add, scale=1.0,
                                scalar=-3.0e38, op0=ALU.add, op1=ALU.max, accum_out=row_max[:, b, q:q + 1])
                        link(done)
                        dve.tensor_scalar(neg_max[:, b, :], row_max[:, b, :], -1.0, None, ALU.mult)\
                            .then_inc(s_taken, 1)
                        if n == HEADS + 1:
                            group_out(0)
                    group_out(1)
                    for h in range(HALVES):
                        xT_low(h, v0)
                    for part in range(2):
                        lo_g(g0 + 8, (g0 + 8) % 2, part)
                    out0, end = g0 + 6, v0 + 2

                if kind == "sgu":
                    dve.wait_ge(sgu_bias_ld, 16)
                    for c in range(4):
                        at = 512 * SGU_ORDER[c]
                        for h in range(HALVES):
                            lo_g(g0 + c + 1, (g0 + c + 1) % 2, h)
                            dve.wait_ge(g_done, 2 * (g0 + c) + h + 1)
                            if c >= 1:
                                dve.wait_ge(act_done, a0 + 2 * (c - 1) + h + 1)
                            dve.tensor_tensor(stage[:, h, :], gu[h][:, :], bias_tab[:, at:at + 512], ALU.add)\
                                .then_inc(gu_taken[h], 1)
                        if c >= 2:
                            h = c - 2
                            dve.wait_ge(act_done, a0 + 2 + h + 1)
                            normalise(v_sgu[:, h, :], v_sgu[:, h, :], h, ln0, vn_ready)
                    for h in range(HALVES):
                        dve.wait_ge(mix_done, h + 1)
                        if h == 0:
                            dve.wait_ge(act_done, a0 + 8)
                        for g in range(HEADS):
                            cols = slice(P * g, P * g + P)
                            done = dve.scalar_tensor_tensor(
                                out=t_tok[:, h, cols], in0=acc[h][:, g // 4, P * (g % 4):P * (g % 4) + P],
                                scalar=bs_col[:, g:g + 1], in1=u_sgu[:, h, cols], op0=ALU.add, op1=ALU.mult)
                            if g % 4 == 3:
                                done.then_inc(tok_ready, 1)
                    for h in range(HALVES):
                        xT_low(h, v0)
                    for j in range(2):
                        for part in range(2):
                            lo_g(g0 + 5 + j, (g0 + 5 + j) % 2, part)
                    ln0, out0, end = ln0 + 1, g0 + 4, v0 + 2

                if kind in ("attn", "sgu"):
                    for h in range(HALVES):
                        residual_norm(h, ln0, r0, [(g_done, 2 * (out0 + j) + h + 1) for j in range(2)])
                        xT_low(h, end)

        @block.gpsimd
        def _(pool):
            pool.memset(ident[:, :], 0.0).then_inc(pool_step, 1)
            pool.wait_ge(pool_step, 1)
            pool.affine_select(out=ident[:, :], in_=ident[:, :], compare_op=ALU.not_equal, fill=1.0, base=0,
                               pattern=[[-1, P]], channel_multiplier=1).then_inc(const_ready, 1)
            pool.memset(flip[:, :], 0.0).then_inc(pool_step, 1)
            pool.wait_ge(pool_step, 2)
            pool.affine_select(out=flip[:, :], in_=flip[:, :], compare_op=ALU.not_equal, fill=1.0, base=1 - P,
                               pattern=[[1, P]], channel_multiplier=1).then_inc(const_ready, 1)
            pool.dma_start(rel_sb[:, :], rel_bias).then_inc(bias_in, 16)
            pool.dma_start(onehot_sb, bucket_onehot).then_inc(bias_in, 16)
            pool.memset(neg_half, -0.5).then_inc(pool_step, 1)

            def load_ln(ln):
                g, b = [(ln_g[i, s], ln_b[i, s]) for i, s in ((0, 0), (0, 1), (0, 2), (1, 0))][ln] if ln < 4 \
                    else ((sgu_ln_g[0], sgu_ln_b[0]), (ln_g[1, 1], ln_b[1, 1]), (ln_g[1, 2], ln_b[1, 2]))[ln - 4]
                for dst, src in ((gamma, g), (beta, b)):
                    pool.dma_start(dst[:, :], src.partition_broadcast(P)).then_inc(ln_loaded, 16)

            load_ln(0)
            with nc.allow_non_contiguous_dma(reason="eight columns, once"):
                pool.dma_start(wf_raw[:, :, :], attn_w_in[0].rearrange("(b p) n -> p b n", p=P)
                               [:, :, 6 * 512:6 * 512 + HEADS]).then_inc(f_loaded, 16)
                pool.dma_start(bs_col, sgu_b_s[0].rearrange("g t -> t g")).then_inc(rows_loaded, 16)
            pool.dma_start(bf_row, attn_b_f[0].partition_broadcast(P)).then_inc(rows_loaded, 16)
            pool.dma_start(p_tok[:, :, :], p_in[0, 0].rearrange("(h p) n -> p h n", p=P)).then_inc(p_loaded, 16)
            pool.memset(causal[:, :], 0.0).then_inc(pool_step, 1)
            pool.memset(sel[:, :], 0.0).then_inc(pool_step, 1)
            pool.wait_ge(pool_step, 5)
            pool.affine_select(out=causal[:, :], in_=causal[:, :], compare_op=ALU.is_ge, fill=NEG, base=P,
                               pattern=[[-1, S]], channel_multiplier=1).then_inc(const_ready, 1)
            sel_v = sel[:, :].rearrange("p (n t) -> p n t", t=P)
            pool.affine_select(out=sel_v, in_=sel_v, compare_op=ALU.not_equal, fill=1.0, base=0,
                               pattern=[[-1, HEADS], [0, P]], channel_multiplier=1).then_inc(const_ready, 1)
            pool.wait_ge(bias_sb, 1)
            pool.dma_start(bias_rows, bias_row_sb).then_inc(bias_st, 16)
            pool.wait_ge(bias_st, 16)
            ln_end = []
            for k, (kind, _, _) in enumerate(PHASES):
                if kind == "ffn":
                    ln_end.append((tok_ready, bases[k]["x"] + 4))
                elif kind == "sgu":
                    ln_end.append((vn_ready, 4))
                if kind in ("attn", "sgu"):
                    ln_end.append((tok_ready, bases[k]["x"] + 8))
            for ln in range(total["ln"]):
                for h in range(HALVES):
                    pool.wait_ge(var_ready, 2 * ln + h + 1)
                    pool.tensor_tensor(rstd[:, h:h + 1], var_eps[:, h:h + 1], neg_half, ALU.pow)\
                        .then_inc(rstd_ready, 1)
                if ln == 0:
                    pool.wait_ge(d_done, 2 * NCH)
                    pool.dma_start(bias_rev[:, :, :].rearrange("p h (n u) -> p (h n) u", u=S),
                                   bass.AP(bias_rows.tensor, 0, [[1, P], [512, HEADS], [1, S]]))\
                        .then_inc(bias_ld, 16)
                if ln == 2:
                    pool.dma_start(bias_tab[:, :], sgu_b_in[0].partition_broadcast(P)).then_inc(sgu_bias_ld, 16)
                if ln == 3:
                    pool.dma_start(ws_tok[:, :, :], sgu_w_s[0].rearrange("g t s -> t g s"))\
                        .then_inc(ws_raw, 16)
                    pool.wait_ge(ws_raw, 16)
                    pool.affine_select(out=ws_tok[:, :, :], in_=ws_tok[:, :, :], compare_op=ALU.is_ge, fill=0.0,
                                       base=0, pattern=[[0, HEADS], [-1, P]], channel_multiplier=1)\
                        .then_inc(ws_loaded, 1)
                    pool.dma_start(p_tok[:, :, :], p_in[1, 0].rearrange("(h p) n -> p h n", p=P))\
                        .then_inc(p_loaded, 16)
                if ln + 1 < total["ln"]:
                    pool.wait_ge(*ln_end[ln])
                    load_ln(ln + 1)


def bucket_of(n):
    exact = BUCKETS // 2
    if n < exact:
        return n
    big = exact + int(np.float32(np.log(np.float32(n / exact))) / np.float32(math.log(128 / exact))
                      * np.float32(BUCKETS - exact))
    return min(big, BUCKETS - 1)


_INS = ["x", "p", "ln_g", "ln_b", "ffn_w_gate", "ffn_w_up", "ffn_w_down", "attn_w_in", "attn_b_f", "attn_w_out",
        "rel_bias", "sgu_w_in", "sgu_b_in", "sgu_ln_g", "sgu_ln_b", "sgu_w_s", "sgu_b_s", "sgu_w_out",
        "ple_w_proj", "ple_w_gate"]


def kernel(**inputs):
    import concourse.bacc as bacc
    from concourse.bass_utils import run_bass_kernel_spmd

    nc = bacc.Bacc("TRN2", target_bir_lowering=False, num_devices=1)
    onehot = np.zeros((BUCKETS, 512), np.float32)
    for j in range(S):
        onehot[bucket_of(S - 1 - j), j] = 1.0
    arrays = {"in_bucket_onehot": onehot}
    args = [nc.dram_tensor("in_bucket_onehot", onehot.shape, F32, kind="ExternalInput").ap()]
    for name in _INS:
        a = np.ascontiguousarray(inputs[name])
        arrays[f"in_{name}"] = a
        args.append(nc.dram_tensor(f"in_{name}", a.shape, mybir.dt.from_np(a.dtype), kind="ExternalInput").ap())
    out = nc.dram_tensor("out_0", (1, S, D), F32, kind="ExternalOutput").ap()
    build(nc, *args, out)
    r = run_bass_kernel_spmd(nc, [arrays], core_ids=[0])
    return r.results[0]["out_0"]
```

```python
import math
from contextlib import ExitStack

import numpy as np

import concourse.bass as bass
from concourse import mybir

F32 = mybir.dt.float32
F32R = mybir.dt.float32r
ALU = mybir.AluOpType
ACT = mybir.ActivationFunctionType
AXX = mybir.AxisListType.X

P = 128
D = 1024
S = 256
HALVES = S // P
KB = D // P
FF = 2816
FC = 256
NCH = FF // FC
HD = 64
HEADS = 8
PLE = 256
DEPTH = 2
ALPHA = (2.0 * DEPTH) ** 0.25
EPS = 1e-5
NEG = -1e30
SCALE = HD ** -0.5
BUCKETS = 32
PHASES = [("ffn", 0, 0), ("attn", 0, 1), ("ffn", 0, 2), ("ple", 0, 0),
          ("ffn", 1, 0), ("sgu", 1, 1), ("ffn", 1, 2), ("ple", 1, 0)]
SGU_ORDER = [2, 3, 0, 1]


PAIR = [(0, 0), (1, 0), (0, 1), (1, 1)]
ATTN_ORDER = [
    ("g", 0, 0), ("half1",), ("g", 0, 1), ("turn", 0, 0), ("forget",),
    ("g", 1, 0), ("turn", 0, 1), ("zT",), ("g", 1, 1), ("turn", 1, 0),
    ("g", 2, 0), ("turn", 1, 1), ("cT",), ("g", 2, 1),
    ("g", 3, 0), ("head", 0), ("g", 3, 1), ("turn", 3, 0), ("head", 1),
    ("g", 4, 0), ("turn", 3, 1), ("head", 2), ("g", 4, 1), ("turn", 4, 0), ("head", 3), ("head", 4),
    ("g", 5, 0), ("turn", 4, 1), ("head", 5), ("head", 6), ("g", 5, 1), ("head", 7), ("head", 8),
] + [("head", n) for n in range(9, 2 * 8 + 2)]


def attn_tp_uses():
    uses, count = {}, [0, 0]
    for e in ATTN_ORDER:
        if e[0] == "turn":
            key, bank = e, e[2]
        elif e[0] in ("zT", "cT"):
            key, bank = e, ("zT", "cT").index(e[0])
        elif e[0] == "head" and e[1] >= 1 and e[1] <= 2 * HEADS:
            key, bank = ("probs", e[1] - 1), (e[1] - 1) % 2
        else:
            continue
        uses[key] = (bank, count[bank])
        count[bank] += 1
    return uses


def phase_bases():
    per = {"ffn": dict(g=NCH, d=NCH, u=NCH, t=NCH + 2, v=NCH + 2, a=2 * NCH, x=4, r=4, ln=1),
           "attn": dict(g=8, d=0, u=6, t=5 + HEADS + 2 + 2, v=4, a=0, x=8, r=4, ln=1),
           "sgu": dict(g=6, d=0, u=4, t=1 + 2 + 2, v=4, a=8, x=8, r=4, ln=2),
           "ple": dict(g=2, d=1, u=2, t=2, v=2, a=4, x=4, r=0, ln=0)}
    now = dict(g=0, d=0, u=0, t=2, v=2, a=0, x=0, r=0, ln=0)
    out = []
    for kind, _, s in PHASES:
        out.append(dict(now))
        now = {k: now[k] + per[kind][k] for k in now}
        if kind == "ffn" and s == 2:
            now["t"] += 1
            now["v"] += 1
    return out, now


def build(nc, bucket_onehot, x_in, p_in, ln_g, ln_b, w_gate, w_up, w_down, attn_w_in, attn_b_f, attn_w_out,
          rel_bias, sgu_w_in, sgu_b_in, sgu_ln_g, sgu_ln_b, sgu_w_s, sgu_b_s, sgu_w_out, ple_w_proj,
          ple_w_gate, out):
    bases, total = phase_bases()
    tp_of = attn_tp_uses()
    pair_firsts = set()
    for k, (kind, _, _) in enumerate(PHASES):
        pair_firsts |= {bases[k]["g"] + q for q in {"ffn": (), "attn": (6,), "sgu": (2, 4), "ple": (0,)}[kind]}

    def g_used(m):
        return 2 * m + 3 if isinstance(m, int) and m in pair_firsts else 2 * m + 2

    bias_rows = nc.dram_tensor("bias_rows", (HEADS, 512), F32, kind="Internal").ap()

    with ExitStack() as ctx:
        def sb(name, shape, dt=F32, where=ctx):
            return where.enter_context(nc.sbuf_tensor(name, shape, dt))

        def sem(name):
            return ctx.enter_context(nc.semaphore(name))

        rawA = sb("rawA", [P, 4, 512])
        rawB = sb("rawB", [P, 4, 512])
        rawD = sb("rawD", [P, 2, D])
        g_hi = sb("g_hi", [P, 2, KB, 512], F32R)
        g_lo = sb("g_lo", [P, 2, KB, 512], F32R)
        x_tok = sb("x_tok", [P, HALVES, D])
        t_tok = sb("t_tok", [P, HALVES, D])
        xT_hi = sb("xT_hi", [P, KB, S], F32R)
        xT_lo = sb("xT_lo", [P, KB, S], F32R)
        stage = sb("stage", [P, HALVES, 512])
        hT_hi = sb("hT_hi", [P, HALVES, 2, P], F32R)
        hT_lo = sb("hT_lo", [P, HALVES, 2, P], F32R)
        gamma = sb("gamma", [P, D])
        beta = sb("beta", [P, D])
        bias_tab = sb("bias_tab", [P, 2048])
        p_tok = sb("p_tok", [P, HALVES, PLE])
        probs = sb("probs", [P, 2, 384])
        logits = sb("logits", [P, 2, 384])
        probsT = sb("probsT", [P, 2, 384])
        ident = sb("ident", [P, P])
        flip = sb("flip", [P, P])
        wf_raw = sb("wf_raw", [P, KB, HEADS])
        wf_hi = sb("wf_hi", [P, KB, HEADS], F32R)
        wf_lo = sb("wf_lo", [P, KB, HEADS], F32R)
        small = sb("small", [P, 256])
        zf = small[:, 0:16].rearrange("p (h n) -> p h n", h=2)
        c_tok = small[:, 16:32].rearrange("p (h n) -> p h n", h=2)
        bf_row = small[:, 32:40]
        row_sum = small[:, 40:72].rearrange("p (i n) -> p i n", i=2)
        row_inv = small[:, 72:104].rearrange("p (i n) -> p i n", i=2)
        row_max = small[:, 104:108].rearrange("p (b i) -> p b i", b=2)
        neg_max = small[:, 108:112].rearrange("p (b i) -> p b i", b=2)
        stats = small[:, 112:136].rearrange("p (h n) -> p h n", h=2)
        mean_var = small[:, 136:140].rearrange("p (h n) -> p h n", h=2)
        var_eps = small[:, 140:142]
        rstd = small[:, 142:144]
        neg_half = small[:, 144:145]
        bs_col = small[:, 152:160]
        with ExitStack() as region:
            d_hi = sb("d_hi", [P, 2, 2, D], F32R, region)
            d_lo = sb("d_lo", [P, 2, 2, D], F32R, region)
        with ExitStack() as region:
            qT = sb("qT", [P, HEADS, S], where=region)
            kT = sb("kT", [P, HEADS, S], where=region)
            v_att = sb("v_att", [P, HALVES, 2 * 512], where=region)
            head_c = sb("head_c", [HEADS, 2048], where=region)
        bias_rev = v_att
        with ExitStack() as region:
            u_sgu = sb("u_sgu", [P, HALVES, D], where=region)
            v_sgu = sb("v_sgu", [P, HALVES, D], where=region)
            ws_tok = sb("ws_tok", [P, HEADS, P], where=region)
            ws_T = sb("ws_T", [P, HEADS, P], where=region)
        region_end = sb("region_tail", [P, 2, 2 * D + 2 * D])
        del region_end
        causal = sb("causal", [P, S])
        causal_c = sb("causal_c", [P, 2, 384])
        sel = sb("sel", [HEADS, HEADS * P])
        rel_sb = sb("rel_sb", [BUCKETS, HEADS])
        onehot_sb = probs[0:BUCKETS, :, :].rearrange("p a b -> p (a b)")[:, 0:512]
        bias_row_sb = logits[0:HEADS, :, :].rearrange("p a b -> p (a b)")[:, 0:512]
        lf = head_c[:, :].rearrange("p (n s) -> p n s", s=S)

        acc = [ctx.enter_context(nc.psum_tensor(f"acc{h}", [P, 2, 512], F32)) for h in range(2)]
        gu = [ctx.enter_context(nc.psum_tensor(f"gu{h}", [P, 512], F32)) for h in range(2)]
        tp = [ctx.enter_context(nc.psum_tensor(f"tp{h}", [P, 512], F32)) for h in range(2)]

        raw_a, raw_b, raw_d = sem("raw_a"), sem("raw_b"), sem("raw_d")
        high_a, high_b, high_d = sem("high_a"), sem("high_b"), sem("high_d")
        split_a, split_b, split_d = sem("split_a"), sem("split_b"), sem("split_d")
        g_done = sem("g_done")
        d_done = sem("d_done")
        gu_taken = [sem("gu_taken0"), sem("gu_taken1")]
        tp_full = [sem("tp_full0"), sem("tp_full1")]
        tp_hi = [sem("tp_hi0"), sem("tp_hi1")]
        tp_taken = [sem("tp_taken0"), sem("tp_taken1")]
        act_done = sem("act_done")
        tok_ready = sem("tok_ready")
        acc_read = sem("acc_read")
        x_loaded, p_loaded = [sem("x_loaded0"), sem("x_loaded1")], sem("p_loaded")
        ln_loaded = sem("ln_loaded")
        var_ready, rstd_ready = sem("var_ready"), sem("rstd_ready")
        step = sem("step")
        const_ready, pool_step = sem("const_ready"), sem("pool_step")
        bias_in, bias_mm, bias_sb, bias_st, bias_ld, bias_flip, bias_done = (
            sem("bias_in"), sem("bias_mm"), sem("bias_sb"), sem("bias_st"), sem("bias_ld"), sem("bias_flip"),
            sem("bias_done"))
        f_loaded, f_hi, f_split, f_mm, f_tok, f_exp, f_arg, f_ln, f_cum = (
            sem("f_loaded"), sem("f_hi"), sem("f_split"), sem("f_mm"), sem("f_tok"), sem("f_exp"),
            sem("f_arg"), sem("f_ln"), sem("f_cum"))
        s_full, s_taken, p_ready, pv_done = sem("s_full"), sem("s_taken"), sem("p_ready"), sem("pv_done")
        ws_loaded, vn_ready, mix_done, sgu_bias_ld, ws_raw = (
            sem("ws_loaded"), sem("vn_ready"), sem("mix_done"), sem("sgu_bias_ld"),
            sem("ws_raw"))
        rows_loaded = sem("rows_loaded")
        out_done = sem("out_done")

        block = ctx.enter_context(nc.Block())

        def g_source(k, c, part):
            kind, i, s = PHASES[k]
            rows = slice(4 * part, 4 * part + 4)
            if kind == "ffn":
                cols = bass.DynSlice(c * FC, FC)
                gate = w_gate[i, s // 2].rearrange("(b p) n -> p b n", p=P)[:, rows, cols]
                up = w_up[i, s // 2].rearrange("(b p) n -> p b n", p=P)[:, rows, cols]
                return [(slice(0, 4), slice(0, FC), gate), (slice(0, 4), slice(FC, 2 * FC), up)]
            if kind == "attn":
                w, c = (attn_w_in[0], c) if c < 6 else (attn_w_out[0], c - 6)
            elif kind == "sgu":
                w, c = (sgu_w_in[0], SGU_ORDER[c]) if c < 4 else (sgu_w_out[0], c - 4)
            else:
                w = ple_w_gate[i]
            v = w.rearrange("(b p) n -> p b n", p=P)[:, rows, 512 * c:512 * c + 512]
            return [(slice(0, 2), slice(0, 512), v[:, 0:2]), (slice(2, 4), slice(0, 512), v[:, 2:4])]

        @block.sync
        def _(sp):
            def load_half(n, k, c, part):
                raw, loaded, split = ((rawA, raw_a, split_a), (rawB, raw_b, split_b))[part]
                if not (isinstance(n, int) and n == 0):
                    sp.wait_ge(split, n)
                for b, cols, src in g_source(k, c, part):
                    sp.dma_start(raw[:, b, cols], src).then_inc(loaded, 16)

            def load_d(m, src):
                if not (isinstance(m, int) and m == 0):
                    sp.wait_ge(split_d, m)
                sp.dma_start(rawD[:, :, :], src).then_inc(raw_d, 16)

            def load_x(h):
                sp.dma_start(x_tok[:, h, :], x_in[0, h * P:(h + 1) * P, :]).then_inc(x_loaded[h], 16)

            load_x(0)
            load_half(0, 0, 0, 0)
            load_half(0, 0, 0, 1)
            load_x(1)
            for k, (kind, i, s) in enumerate(PHASES):
                g0, d0 = bases[k]["g"], bases[k]["d"]
                chunks = {"ffn": NCH, "attn": 8, "sgu": 6, "ple": 2}[kind]

                def load_next(c, part):
                    if c + 1 < chunks:
                        load_half(g0 + c + 1, k, c + 1, part)
                    elif k + 1 < len(PHASES):
                        load_half(g0 + c + 1, k + 1, 0, part)

                if kind == "ffn":
                    down = w_down[i, s // 2].rearrange("(c b p) n -> p c b n", b=2, p=P)
                    load_next(0, 0)
                    load_d(d0, down[:, 0])
                    load_next(0, 1)
                    with sp.Fori(1, NCH - 1) as c:
                        load_half(g0 + 1 + c, k, c + 1, 0)
                        load_d(d0 + c, down[:, bass.DynSlice(c, 1)])
                        load_half(g0 + 1 + c, k, c + 1, 1)
                    load_next(NCH - 1, 0)
                    load_d(d0 + NCH - 1, down[:, NCH - 1])
                    load_next(NCH - 1, 1)
                    if s == 2:
                        load_d(d0 + NCH, ple_w_proj[i].rearrange("(b p) n -> p b n", p=P))
                else:
                    for c in range(chunks):
                        for part in range(2):
                            load_next(c, part)
            for n, (j, h) in enumerate(PAIR):
                sp.wait_ge(tok_ready, bases[-1]["x"] + n + 1)
                sp.dma_start(out[0, h * P:(h + 1) * P, 512 * j:512 * j + 512],
                             x_tok[:, h, 512 * j:512 * j + 512]).then_inc(out_done, 16)
            sp.wait_ge(out_done, 4 * 16)

        @block.tensor
        def _(pe):
            def product(dst, hi, lo, w_hi, w_lo, first=True, last=True):
                for b in range(len(hi)):
                    pe.matmul(dst, hi[b], w_hi[b], start=first and b == 0, stop=False)
                    pe.matmul(dst, hi[b], w_lo[b], start=False, stop=False)
                    done = pe.matmul(dst, lo[b], w_hi[b], start=False, stop=last and b == len(hi) - 1)
                return done

            def g_half(n, slot, h, dst, part):
                tok = slice(h * P, (h + 1) * P)
                if h == 0:
                    pe.wait_ge((split_a, split_b)[part], n + 1)
                ks = range(4 * part, 4 * part + 4)
                return product(dst, [xT_hi[:, b, tok] for b in ks], [xT_lo[:, b, tok] for b in ks],
                               [g_hi[:, slot, b, :] for b in ks], [g_lo[:, slot, b, :] for b in ks],
                               first=part == 0, last=part == 1)

            def g_product(n, slot, h, dst):
                g_half(n, slot, h, dst, 0)
                g_half(n, slot, h, dst, 1).then_inc(g_done, 1)

            def bank_free(bank, uses):
                if not (isinstance(uses, int) and uses == 0):
                    pe.wait_ge(gu_taken[bank], uses)

            def d_product(m, slot, h, first, last):
                pe.wait_ge(split_d, m + 1)
                for j in range(2):
                    cols = slice(512 * j, 512 * j + 512)
                    done = product(acc[h][:, j, :], [hT_hi[:, h, b, :] for b in range(2)],
                                   [hT_lo[:, h, b, :] for b in range(2)],
                                   [d_hi[:, slot, b, cols] for b in range(2)],
                                   [d_lo[:, slot, b, cols] for b in range(2)], first=first, last=last)
                done.then_inc(d_done, 1)

            def transposes(bank, use, srcs):
                if not (isinstance(use, int) and use == 0):
                    pe.wait_ge(tp_taken[bank], use)
                for q, src in enumerate(srcs):
                    rows = src.shape[0]
                    done = pe.transpose(tp[bank][0:src.shape[1], rows * q:rows * q + rows], src,
                                        ident[0:rows, 0:rows])
                done.then_inc(tp_full[bank], 1)

            def token_transposes(src, h, use, needs):
                for j in range(2):
                    pe.wait_ge(*needs[j])
                    transposes(j, use, [src[:, h, 512 * j + P * q:512 * j + P * q + P] for q in range(4)])

            def xT_wait(h, use):
                for j in range(2):
                    pe.wait_ge(tp_taken[j], use + h + 1)

            def ln_turn(h, x0, use):
                token_transposes(x_tok, h, use + h, [(tok_ready, x0 + 2 * h + j + 1) for j in range(2)])

            pe.wait_ge(const_ready, 1)
            use = 0
            token_transposes(x_tok, 0, 0, [(x_loaded[0], 16)] * 2)

            def half1():
                token_transposes(x_tok, 1, 1, [(x_loaded[1], 16)] * 2)

            for k, (kind, i, s) in enumerate(PHASES):
                B = bases[k]
                g0, d0, u0, t0, x0, a0 = (B[q] for q in ("g", "d", "u", "t", "x", "a"))

                if kind == "ffn":
                    def up(c, cs, h):
                        bank_free(h, u0 + c)
                        g_product(g0 + c, (g0 + cs) % 2, h, gu[h][:, :])

                    def turn(c, h):
                        pe.wait_ge(gu_taken[h], u0 + c + 1)
                        transposes(h, t0 + c, [stage[:, h, FC + P * b:FC + P * b + P] for b in range(2)])

                    def down(c, cs, h):
                        pe.wait_ge(tp_taken[h], t0 + c + 1)
                        d_product(d0 + c, (d0 + cs) % 2, h, first=cs == 0, last=cs == NCH - 1)

                    def chunk(c, cs):
                        up(c, cs, 0)
                        turn(c - 1, 1)
                        down(c - 1, cs - 1, 0)
                        up(c, cs, 1)
                        turn(c, 0)
                        down(c - 1, cs - 1, 1)

                    xT_wait(0, use)
                    up(0, 0, 0)
                    half1()
                    xT_wait(1, use)
                    up(0, 0, 1)
                    if k == 0:
                        pe.wait_ge(bias_in, 32)
                        pe.matmul(acc[1][0:HEADS, 1, :], rel_sb[:, :], onehot_sb, start=True,
                                  stop=True).then_inc(bias_mm, 1)
                    turn(0, 0)
                    if k == 0:
                        pe.wait_ge(bias_sb, 1)
                    chunk(1, 1)
                    with pe.Fori(0, (NCH - 3) // 2) as r:
                        for e in range(2):
                            chunk(r * 2 + (2 + e), 2 + e)
                    c = NCH - 1
                    up(c, c, 0)
                    turn(c - 1, 1)
                    down(c - 1, c - 1, 0)
                    turn(c, 0)
                    bank_free(1, u0 + c)
                    g_half(g0 + c, (g0 + c) % 2, 1, gu[1][:, :], 0)
                    down(c, c, 0)
                    g_half(g0 + c, (g0 + c) % 2, 1, gu[1][:, :], 1).then_inc(g_done, 1)
                    down(c - 1, c - 1, 1)
                    turn(c, 1)
                    down(c, c, 1)
                    use = t0 + NCH
                    if s == 2:
                        pe.wait_ge(p_loaded, 16 * (i + 1))
                        for h in range(HALVES):
                            transposes(h, use, [p_tok[:, h, P * b:P * b + P] for b in range(2)])
                        use += 1
                    ln_turn(0, x0, use)

                    def half1(x0=x0, use=use):
                        ln_turn(1, x0, use)

                if kind == "ple":
                    for n, (j, h) in enumerate(PAIR):
                        if n < 2:
                            bank_free(j, u0)
                        else:
                            pe.wait_ge(act_done, a0 + n - 1)
                        if n % 2 == 0:
                            xT_wait(h, use)
                        if n == 3 and k + 1 < len(PHASES):
                            token_transposes(x_tok, 0, t0, [(tok_ready, x0 + 2)] * 2)
                        g_product(g0 + j, (g0 + j) % 2, h, gu[j][:, :])
                        if n == 1:
                            half1()
                            d_product(d0, d0 % 2, 0, first=True, last=True)
                        if n == 2:
                            d_product(d0, d0 % 2, 1, first=True, last=True)
                    use = t0

                    def half1(x0=x0, use=use):
                        token_transposes(x_tok, 1, use + 1, [(tok_ready, x0 + 4)] * 2)

                if kind == "attn":
                    def scores(n):
                        g, hh, sl = n // HEADS, n % HEADS, n % 2
                        rows, blk = slice(HD * (hh % 2), HD * (hh % 2) + HD), 4 * g + hh // 2
                        if n == 0:
                            pe.wait_ge(bias_done, 1)
                        if hh == 0:
                            for b in range(2):
                                pe.wait_ge(tp_taken[b], t0 + tp_of[("turn", 3 * g + 1, b)][1] + 1)
                        if n >= 2:
                            pe.wait_ge(s_taken, n - 1)
                        for i_q, cols in ((1, slice(0, S)), (0, slice(S, S + P))):
                            wide = cols.stop - cols.start
                            dst = acc[0][:, sl, cols]
                            done = pe.matmul(dst, qT[rows, blk, i_q * P:i_q * P + P], kT[rows, blk, 0:wide],
                                             start=True, stop=g == 0)
                            if g == 1:
                                done = pe.matmul(dst, sel[:, hh * P:hh * P + P], lf[:, 1, 0:wide],
                                                 start=False, stop=True)
                        done.then_inc(s_full, 1)

                    def probs_turn(n):
                        pe.wait_ge(p_ready, n + 1)
                        bank, at = tp_of[("probs", n)]
                        transposes(bank, t0 + at, [probs[:, bank, P * q:P * q + P] for q in range(3)])

                    def values(n):
                        g, hh, sl = n // HEADS, n % HEADS, n % 2
                        pe.wait_ge(tp_taken[sl], t0 + tp_of[("probs", n)][1] + 1)
                        if hh == 0:
                            for h in range(HALVES):
                                pe.wait_ge(gu_taken[h], u0 + 3 * (g + 1))
                        if n == HEADS:
                            pe.wait_ge(tok_ready, x0 + 2)
                        vc = slice(g * 512 + hh * HD, g * 512 + hh * HD + HD)
                        oc = slice(hh * HD, hh * HD + HD)
                        pe.matmul(acc[1][:, 0, oc], probsT[:, sl, 2 * P:3 * P], v_att[:, 0, vc],
                                  start=True, stop=True)
                        pe.matmul(acc[1][:, 1, oc], probsT[:, sl, 0:P], v_att[:, 0, vc], start=True, stop=False)
                        pe.matmul(acc[1][:, 1, oc], probsT[:, sl, P:2 * P], v_att[:, 1, vc],
                                  start=False, stop=True).then_inc(pv_done, 1)

                    for e in ATTN_ORDER:
                        if e[0] == "g":
                            c, h = e[1:]
                            if c == 0:
                                xT_wait(h, use)
                            bank_free(h, u0 + c)
                            g_product(g0 + c, (g0 + c) % 2, h, gu[h][:, :])
                        elif e[0] == "half1":
                            half1()
                        elif e[0] == "turn":
                            c, h = e[1:]
                            pe.wait_ge(gu_taken[h], u0 + c + 1)
                            transposes(h, t0 + tp_of[e][1], [stage[:, h, P * q:P * q + P] for q in range(4)])
                        elif e[0] == "forget":
                            pe.wait_ge(f_split, 1)
                            for h in range(HALVES):
                                tok = slice(h * P, (h + 1) * P)
                                done = product(acc[h][:, 0, 0:HEADS], [xT_hi[:, b, tok] for b in range(KB)],
                                               [xT_lo[:, b, tok] for b in range(KB)],
                                               [wf_hi[:, b, :] for b in range(KB)],
                                               [wf_lo[:, b, :] for b in range(KB)])
                                done.then_inc(f_mm, 1)
                        elif e[0] == "zT":
                            pe.wait_ge(f_tok, 2)
                            transposes(0, t0 + tp_of[e][1], [zf[:, h, :] for h in range(2)])
                            pe.wait_ge(bias_ld, 16)
                            for q in range(4):
                                done = pe.matmul(acc[q // 2][:, q % 2, :], flip[:, :],
                                                 bias_rev[:, q // 2, 512 * (q % 2):512 * (q % 2) + 512],
                                                 start=True, stop=True)
                            done.then_inc(bias_flip, 1)
                        elif e[0] == "cT":
                            pe.wait_ge(f_cum, 1)
                            pe.wait_ge(tp_taken[1], t0 + tp_of[e][1])
                            for h in range(2):
                                done = pe.transpose(tp[1][:, HEADS * h:HEADS * h + HEADS],
                                                    lf[:, 0, h * P:(h + 1) * P], ident[0:HEADS, 0:HEADS])
                            done.then_inc(tp_full[1], 1)
                        else:
                            n = e[1]
                            if n < 2 * HEADS:
                                scores(n)
                            if 1 <= n <= 2 * HEADS:
                                probs_turn(n - 1)
                            if n >= 2:
                                values(n - 2)
                    use = t0 + 5 + HEADS
                    for h in range(HALVES):
                        token_transposes(t_tok, h, use + h, [(tok_ready, x0 + 2 + h + 1)] * 2)
                    out0, y_turn = g0 + 6, None

                if kind == "sgu":
                    def mix(h):
                        pe.wait_ge(vn_ready, 2 * (h + 1))
                        for g in range(HEADS):
                            done = pe.matmul(acc[h][:, g // 4, P * (g % 4):P * (g % 4) + P], ws_T[:, g, :],
                                             v_sgu[:, h, P * g:P * g + P], start=True, stop=True)
                        done.then_inc(mix_done, 1)

                    def y_turn(h):
                        token_transposes(t_tok, h, t0 + 1 + h, [(tok_ready, x0 + 2 * h + j + 1) for j in range(2)])

                    for n, (c, h) in enumerate([(0, 0), (0, 1), (1, 0), (1, 1)] + [(2 + j, h) for j, h in PAIR]):
                        if c == 0:
                            xT_wait(h, use)
                        bank_free(n % 2, u0 + n // 2)
                        g_product(g0 + c, (g0 + c) % 2, h, gu[n % 2][:, :])
                        if n == 0:
                            half1()
                        if n == 1:
                            pe.wait_ge(ws_loaded, 1)
                            for b in range(2):
                                transposes(b, t0, [ws_tok[:, 4 * b + q, :] for q in range(4)])
                        if n == 5:
                            for b in range(2):
                                pe.wait_ge(tp_taken[b], t0 + 1)
                            mix(0)
                        if n == 6:
                            y_turn(0)
                        if n == 7:
                            mix(1)
                    use, out0 = t0 + 1, g0 + 4

                if kind in ("attn", "sgu"):
                    for n, (j, h) in enumerate(PAIR):
                        if n == 2 and y_turn is not None:
                            y_turn(1)
                        if n % 2 == 0:
                            xT_wait(h, use)
                        if n == 3:
                            ln_turn(0, x0 + 4, use + 2)
                        g_product(out0 + j, (out0 + j) % 2, h, acc[h][:, j, :])
                    use += 2

                    def half1(x0=x0 + 4, use=use):
                        ln_turn(1, x0, use)

        @block.scalar
        def _(act):
            def copy(dst, src, scale=1.0):
                return act.activation(dst, src, ACT.Copy, scale=scale)

            def hi_g(n, part):
                raw, loaded, done = ((rawA, raw_a, high_a), (rawB, raw_b, high_b))[part]
                hi_g_into(n, n % 2, part)

            def hi_g_into(n, slot, part):
                raw, loaded, done = ((rawA, raw_a, high_a), (rawB, raw_b, high_b))[part]
                act.wait_ge(loaded, 32 * n + 32)
                if not (isinstance(n, int) and n < 2):
                    act.wait_ge(g_done, g_used(n - 2))
                copy(g_hi[:, slot, 4 * part:4 * part + 4, :], raw[:, :, :]).then_inc(done, 1)

            def hi_d(m, slot, free=None):
                act.wait_ge(raw_d, 16 * m + 16)
                if not (isinstance(m, int) and m < 2):
                    act.wait_ge(d_done, 2 * m - 2 if free is None else free)
                copy(d_hi[:, slot, :, :], rawD[:, :, :]).then_inc(high_d, 1)

            def xT_high(h, use):
                for j in range(2):
                    act.wait_ge(tp_full[j], use + h + 1)
                    copy(xT_hi[:, 4 * j:4 * j + 4, h * P:(h + 1) * P],
                         tp[j][:, :].rearrange("p (b t) -> p b t", b=4)).then_inc(tp_hi[j], 1)

            def hT_high(h, use):
                act.wait_ge(tp_full[h], use + 1)
                copy(hT_hi[:, h, :, :], tp[h][:, 0:2 * P].rearrange("p (b t) -> p b t", b=2)).then_inc(tp_hi[h], 1)

            xT_high(0, 0)
            hi_g(0, 0)
            hi_g(0, 1)

            def half1():
                xT_high(1, 0)

            for k, (kind, i, s) in enumerate(PHASES):
                B = bases[k]
                g0, d0, u0, t0, x0, a0 = (B[q] for q in ("g", "d", "u", "t", "x", "a"))
                last_phase = k + 1 == len(PHASES)

                if kind == "ffn":
                    def gate(c, h, value=None):
                        act.wait_ge(g_done, 2 * c + (2 * g0 + h + 1))
                        act.activation(stage[:, h, 0:FC], gu[h][:, 0:FC], ACT.Silu).then_inc(act_done, 1)

                    def chunk(c, cs):
                        slot = (g0 + cs + 1) % 2
                        hi_g_into(c + (g0 + 1), slot, 0)
                        gate(c, 0)
                        if cs > 0:
                            hT_high(1, c + (t0 - 1))
                        else:
                            half1()
                        hi_d(c + d0, (d0 + cs) % 2)
                        hi_g_into(c + (g0 + 1), slot, 1)
                        gate(c, 1)
                        hT_high(0, c + t0)

                    chunk(0, 0)
                    chunk(1, 1)
                    with act.Fori(0, (NCH - 3) // 2) as r:
                        for e in range(2):
                            chunk(r * 2 + (2 + e), 2 + e)
                    c = NCH - 1
                    hi_g(g0 + NCH, 0)
                    hi_d(d0 + c, (d0 + c) % 2)
                    gate(c, 0)
                    hT_high(1, t0 + c - 1)
                    hT_high(0, t0 + c)
                    hi_g(g0 + NCH, 1)
                    gate(c, 1)
                    hT_high(1, t0 + c)
                    use = t0 + NCH
                    if s == 2:
                        for h in range(HALVES):
                            hT_high(h, use)
                        use += 1
                    if k == 0:
                        act.wait_ge(f_loaded, 16)
                        copy(wf_hi[:, :, :], wf_raw[:, :, :]).then_inc(f_hi, 1)
                    xT_high(0, use)

                    def half1(use=use):
                        xT_high(1, use)

                if kind == "ple":
                    for part in range(2):
                        hi_g(g0 + 1, part)
                    hi_d(d0, d0 % 2, free=2 * (d0 - 2) + 3)
                    for n, (j, h) in enumerate(PAIR):
                        if n == 2:
                            half1()
                        act.wait_ge(g_done, 2 * g0 + n + 1)
                        if n >= 2:
                            act.wait_ge(tok_ready, x0 + n - 1)
                        act.activation(stage[:, j, :], gu[j][:, :], ACT.Sigmoid).then_inc(act_done, 1)
                        if n == 2 and not last_phase:
                            hi_g(g0 + 2, 0)
                            xT_high(0, t0)
                            hi_g(g0 + 2, 1)

                    def half1(use=t0):
                        xT_high(1, use)

                if kind == "attn":
                    for e in ATTN_ORDER:
                        if e[0] == "g":
                            c, h = e[1:]
                            hi_g(g0 + c + 1, h)
                            act.wait_ge(g_done, 2 * (g0 + c) + h + 1)
                            if c % 3 == 2:
                                g = c // 3
                                copy(v_att[:, h, 512 * g:512 * g + 512], gu[h][:, :]).then_inc(gu_taken[h], 1)
                            else:
                                if c > 0:
                                    before = {1: 0, 3: 1, 4: 3}[c]
                                    act.wait_ge(tp_full[h], t0 + tp_of[("turn", before, h)][1] + 1)
                                copy(stage[:, h, :], gu[h][:, :], SCALE if c % 3 == 0 else 1.0)\
                                    .then_inc(gu_taken[h], 1)
                        elif e[0] == "half1":
                            half1()
                        elif e[0] == "cT":
                            act.wait_ge(f_arg, 1)
                            act.activation(lf[:, 3, :], lf[:, 2, :], ACT.Exp).then_inc(f_exp, 1)
                            act.wait_ge(f_arg, 2)
                            act.activation(lf[:, 5, :], lf[:, 4, :], ACT.Ln).then_inc(f_ln, 1)
                        elif e[0] == "head":
                            n = e[1]
                            if n < 2 * HEADS:
                                b = n % 2
                                act.wait_ge(s_taken, n + 1)
                                for q, cols in ((0, slice(0, S)), (1, slice(S, S + P))):
                                    done = act.activation(probs[:, b, cols], logits[:, b, cols], ACT.Exp,
                                                          bias=neg_max[:, b, q:q + 1],
                                                          accum_out=row_sum[:, 1 - q, n:n + 1])
                                done.then_inc(p_ready, 1)
                            if 1 <= n <= 2 * HEADS:
                                b, at = tp_of[("probs", n - 1)]
                                act.wait_ge(tp_full[b], t0 + at + 1)
                                if n >= 3:
                                    act.wait_ge(pv_done, n - 2)
                                copy(probsT[:, b, :], tp[b][:, 0:384]).then_inc(tp_taken[b], 1)
                            if n in (9, 10):
                                hi_g(g0 + 7, n - 9)
                    for h in range(HALVES):
                        xT_high(h, t0 + 5 + HEADS)
                    after, end = g0 + 8, t0 + 5 + HEADS + 2

                if kind == "sgu":
                    def gelu(n, dst, cols):
                        act.wait_ge(gu_taken[n % 2], u0 + n // 2 + 1)
                        act.activation(dst[:, cols[0], 512 * cols[1]:512 * cols[1] + 512], stage[:, n % 2, :],
                                       ACT.Gelu_apprx_tanh).then_inc(act_done, 1)

                    for n, (c, h) in enumerate([(0, 0), (0, 1), (1, 0), (1, 1)]):
                        hi_g(g0 + c + 1, h)
                        if n == 0:
                            half1()
                        gelu(n, v_sgu, (h, c))
                        if n == 1:
                            for b in range(2):
                                act.wait_ge(tp_full[b], t0 + 1)
                                copy(ws_T[:, 4 * b:4 * b + 4, :],
                                     tp[b][:, :].rearrange("p (b t) -> p b t", b=4)).then_inc(tp_taken[b], 1)
                    for part in range(2):
                        hi_g(g0 + 3, part)
                    for n, (j, h) in enumerate(PAIR):
                        gelu(4 + n, u_sgu, (h, j))
                        if n == 2:
                            hi_g(g0 + 4, 0)
                            xT_high(0, t0 + 1)
                            hi_g(g0 + 4, 1)
                    for part in range(2):
                        hi_g(g0 + 5, part)
                    xT_high(1, t0 + 1)
                    after, end = g0 + 6, t0 + 3

                if kind in ("attn", "sgu"):
                    hi_g(after, 0)
                    xT_high(0, end)
                    hi_g(after, 1)

                    def half1(use=end):
                        xT_high(1, use)

        @block.vector
        def _(dve):
            steps = [0]

            def link(instruction):
                instruction.then_inc(step, 1)
                steps[0] += 1
                dve.wait_ge(step, steps[0])

            def low(dst, src, hi):
                return dve.tensor_tensor(dst, src, hi.bitcast(F32), ALU.subtract)

            def lo_g_into(n, slot, part):
                raw, high, done = ((rawA, high_a, split_a), (rawB, high_b, split_b))[part]
                ks = slice(4 * part, 4 * part + 4)
                dve.wait_ge(high, n + 1)
                low(g_lo[:, slot, ks, :], raw[:, :, :], g_hi[:, slot, ks, :]).then_inc(done, 1)

            def lo_g(n, part):
                lo_g_into(n, n % 2, part)

            def lo_d(m, slot):
                dve.wait_ge(high_d, m + 1)
                low(d_lo[:, slot, :, :], rawD[:, :, :], d_hi[:, slot, :, :]).then_inc(split_d, 1)

            def xT_low(h, use):
                for j in range(2):
                    dve.wait_ge(tp_hi[j], use + h + 1)
                    part = (slice(None), slice(4 * j, 4 * j + 4), slice(h * P, (h + 1) * P))
                    low(xT_lo[part], tp[j][:, :].rearrange("p (b t) -> p b t", b=4), xT_hi[part])\
                        .then_inc(tp_taken[j], 1)

            def hT_low(h, use):
                dve.wait_ge(tp_hi[h], use + 1)
                low(hT_lo[:, h, :, :], tp[h][:, 0:2 * P].rearrange("p (b t) -> p b t", b=2), hT_hi[:, h, :, :])\
                    .then_inc(tp_taken[h], 1)

            def ln_stats(src, h):
                for j in range(2):
                    done = dve.bn_stats(stats[:, h, 6 * j:6 * j + 6], src[:, 512 * j:512 * j + 512])
                link(done)
                link(dve.bn_aggr(mean_var[:, h, :], stats[:, h, :]))
                dve.tensor_scalar(var_eps[:, h:h + 1], mean_var[:, h, 1:2], EPS, None, ALU.add)\
                    .then_inc(var_ready, 1)

            def ln_apply(src, dst, h, ln, j, ready):
                if j == 0:
                    dve.wait_ge(rstd_ready, 2 * ln + h + 1)
                    if h == 0:
                        dve.wait_ge(ln_loaded, 32 * (ln + 1))
                cols = slice(512 * j, 512 * j + 512)
                link(dve.tensor_scalar(src[:, cols], src[:, cols], mean_var[:, h, 0:1], rstd[:, h:h + 1],
                                       ALU.subtract, ALU.mult))
                link(dve.tensor_tensor(src[:, cols], src[:, cols], gamma[:, cols], ALU.mult))
                dve.tensor_tensor(dst[:, cols], src[:, cols], beta[:, cols], ALU.add).then_inc(ready, 1)

            def residual_stats(h, r0, done):
                dve.wait_ge(*done)
                for j in range(2):
                    dve.scalar_tensor_tensor(out=t_tok[:, h, 512 * j:512 * j + 512],
                                             in0=x_tok[:, h, 512 * j:512 * j + 512], scalar=ALPHA,
                                             in1=acc[h][:, j, :], op0=ALU.mult, op1=ALU.add)\
                        .then_inc(acc_read, 1)
                dve.wait_ge(acc_read, r0 + 2 * h + 2)
                ln_stats(t_tok[:, h, :], h)

            def x_apply(h, ln, j):
                ln_apply(t_tok[:, h, :], x_tok[:, h, :], h, ln, j, tok_ready)

            def norm_half1(r0, ln, done, use):
                residual_stats(1, r0, done)
                for j in range(2):
                    x_apply(1, ln, j)
                xT_low(1, use)

            xT_low(0, 0)
            lo_g(0, 0)
            lo_g(0, 1)
            light = True

            def half1():
                xT_low(1, 0)

            for k, (kind, i, s) in enumerate(PHASES):
                B = bases[k]
                g0, d0, u0, t0, v0, a0, x0, r0, ln0 = (B[q] for q in ("g", "d", "u", "t", "v", "a", "x", "r", "ln"))
                last_phase = k + 1 == len(PHASES)

                if kind == "ffn":
                    def gated(c, h):
                        dve.wait_ge(act_done, 2 * c + (a0 + h + 1))
                        dve.scalar_tensor_tensor(out=stage[:, h, FC:2 * FC], in0=stage[:, h, 0:FC], scalar=0.5,
                                                 in1=gu[h][:, FC:2 * FC], op0=ALU.mult, op1=ALU.mult)\
                            .then_inc(gu_taken[h], 1)

                    def chunk(c, cs):
                        slot = (g0 + cs + 1) % 2
                        if cs == 0 and not light:
                            half1()
                            gated(c, 0)
                        lo_g_into(c + (g0 + 1), slot, 0)
                        if cs == 0 and light:
                            half1()
                            gated(c, 0)
                        if cs > 0:
                            gated(c, 0)
                            hT_low(1, c + (v0 - 1))
                        lo_d(c + d0, (d0 + cs) % 2)
                        lo_g_into(c + (g0 + 1), slot, 1)
                        gated(c, 1)
                        hT_low(0, c + v0)

                    chunk(0, 0)
                    if k == 0:
                        dve.wait_ge(bias_mm, 1)
                        link(dve.tensor_copy(bias_row_sb, acc[1][0:HEADS, 1, :]))
                        dve.memset(bias_row_sb[:, S:512], NEG).then_inc(bias_sb, 1)
                    chunk(1, 1)
                    with dve.Fori(0, (NCH - 3) // 2) as r:
                        for e in range(2):
                            chunk(r * 2 + (2 + e), 2 + e)
                    c = NCH - 1
                    lo_g(g0 + NCH, 0)
                    lo_d(d0 + c, (d0 + c) % 2)
                    gated(c, 0)
                    hT_low(1, v0 + c - 1)
                    hT_low(0, v0 + c)
                    lo_g(g0 + NCH, 1)
                    residual_stats(0, r0, (d_done, 2 * (d0 + c)))
                    gated(c, 1)
                    x_apply(0, ln0, 0)
                    hT_low(1, v0 + c)
                    x_apply(0, ln0, 1)
                    use = v0 + NCH
                    if s == 2:
                        for h in range(HALVES):
                            hT_low(h, use)
                        use += 1
                    if k == 0:
                        dve.wait_ge(f_hi, 1)
                        low(wf_lo[:, :, :], wf_raw[:, :, :], wf_hi[:, :, :]).then_inc(f_split, 1)
                    xT_low(0, use)
                    light = False

                    def half1(r0=r0, ln=ln0, done=(d_done, 2 * (d0 + NCH)), use=use):
                        norm_half1(r0, ln, done, use)

                if kind == "ple":
                    for part in range(2):
                        lo_g(g0 + 1, part)
                    half1()
                    lo_d(d0, d0 % 2)
                    for n, (j, h) in enumerate(PAIR):
                        cols = slice(512 * j, 512 * j + 512)
                        if n == 2 and not last_phase:
                            lo_g(g0 + 2, 0)
                        if n % 2 == 0:
                            dve.wait_ge(d_done, 2 * d0 + h + 1)
                        dve.wait_ge(act_done, a0 + n + 1)
                        dve.tensor_tensor(stage[:, j, :], stage[:, j, :], acc[h][:, j, :], ALU.mult)\
                            .then_inc(gu_taken[j], 1)
                        dve.wait_ge(gu_taken[j], u0 + n // 2 + 1)
                        dve.tensor_tensor(x_tok[:, h, cols], x_tok[:, h, cols], stage[:, j, :], ALU.add)\
                            .then_inc(tok_ready, 1)
                        if n == 2 and not last_phase:
                            xT_low(0, v0)
                            lo_g(g0 + 2, 1)
                    light = True

                    def half1(use=v0):
                        xT_low(1, use)

                if kind == "attn":
                    def group_out(g):
                        dve.wait_ge(pv_done, HEADS * (g + 1))
                        cols = slice(HEADS * g, HEADS * g + HEADS)
                        link(dve.reciprocal(row_inv[:, :, cols], row_sum[:, :, cols]))
                        for q in range(2):
                            dve.tensor_tensor(
                                t_tok[:, q, 512 * g:512 * g + 512].rearrange("p (n d) -> p n d", d=HD),
                                acc[1][:, q, :].rearrange("p (n d) -> p n d", d=HD),
                                row_inv[:, q, cols].unsqueeze(2).to_broadcast([P, HEADS, HD]),
                                ALU.mult).then_inc(tok_ready, 1)

                    half1()
                    for e in ATTN_ORDER:
                        if e[0] == "g":
                            lo_g(g0 + e[1] + 1, e[2])
                        elif e[0] == "turn":
                            c, h = e[1:]
                            dst, g, at = (qT, kT)[c % 3], c // 3, tp_of[e][1]
                            dve.wait_ge(tp_full[h], t0 + at + 1)
                            dve.tensor_copy(dst[:, 4 * g:4 * g + 4, h * P:(h + 1) * P],
                                            tp[h][:, :].rearrange("p (b t) -> p b t", b=4)).then_inc(tp_taken[h], 1)
                        elif e[0] == "forget":
                            dve.wait_ge(rows_loaded, 32)
                            for h in range(HALVES):
                                dve.wait_ge(f_mm, h + 1)
                                dve.tensor_tensor(zf[:, h, :], acc[h][:, 0, 0:HEADS], bf_row, ALU.add)\
                                    .then_inc(f_tok, 1)
                        elif e[0] == "zT":
                            at = tp_of[e][1]
                            dve.wait_ge(tp_full[0], t0 + at + 1)
                            dve.tensor_copy(lf[:, 6, :], tp[0][0:HEADS, 0:S]).then_inc(tp_taken[0], 1)
                            dve.wait_ge(tp_taken[0], t0 + at + 1)
                            link(dve.tensor_scalar(lf[:, 7, :], lf[:, 6, :], -1.0, None, ALU.mult))
                            dve.tensor_tensor(lf[:, 2, :], lf[:, 6, :], lf[:, 7, :], ALU.min).then_inc(f_arg, 1)
                            dve.wait_ge(bias_flip, 1)
                            for q in range(4):
                                done = dve.tensor_copy(bias_tab[:, 512 * q:512 * q + 512],
                                                       acc[q // 2][:, q % 2, :])
                            done.then_inc(bias_done, 1)
                        elif e[0] == "cT":
                            dve.wait_ge(f_exp, 1)
                            link(dve.tensor_scalar(lf[:, 4, :], lf[:, 3, :], 1.0, None, ALU.add))
                            dve.tensor_scalar(lf[:, 7, :], lf[:, 4, :], -1.0, None, ALU.add).then_inc(f_arg, 1)
                            dve.wait_ge(f_arg, 2)
                            link(dve.tensor_tensor(lf[:, 7, :], lf[:, 3, :], lf[:, 7, :], ALU.subtract))
                            link(dve.reciprocal(lf[:, 0, :], lf[:, 4, :]))
                            link(dve.tensor_tensor(lf[:, 7, :], lf[:, 7, :], lf[:, 0, :], ALU.mult))
                            dve.wait_ge(f_ln, 1)
                            link(dve.tensor_tensor(lf[:, 5, :], lf[:, 5, :], lf[:, 7, :], ALU.add))
                            link(dve.tensor_scalar(lf[:, 7, :], lf[:, 6, :], 0.0, None, ALU.min))
                            link(dve.tensor_tensor(lf[:, 7, :], lf[:, 7, :], lf[:, 5, :], ALU.subtract))
                            link(dve.memset(lf[:, 2, :], 1.0))
                            link(dve.tensor_tensor_scan(lf[:, 0, :], lf[:, 2, :], lf[:, 7, :], 0.0,
                                                        ALU.mult, ALU.add))
                            dve.tensor_scalar(lf[:, 1, :], lf[:, 0, :], -1.0, None, ALU.mult).then_inc(f_cum, 1)
                            at = tp_of[e][1]
                            dve.wait_ge(tp_full[1], t0 + at + 1)
                            dve.tensor_copy(c_tok[:, :, :], tp[1][:, 0:2 * HEADS]
                                            .rearrange("p (h n) -> p h n", h=2)).then_inc(tp_taken[1], 1)
                        elif e[0] == "head":
                            n = e[1]
                            if n < 2 * HEADS:
                                g, hh, b = n // HEADS, n % HEADS, n % 2
                                pieces = ((0, slice(0, S), 0), (1, slice(S, S + P), P))
                                if n == 0:
                                    dve.wait_ge(bias_done, 1)
                                if n == HEADS:
                                    dve.wait_ge(tp_taken[1], t0 + tp_of[("cT",)][1] + 1)
                                if g == 1:
                                    for q, cols, at in pieces:
                                        done = dve.tensor_scalar(causal_c[:, b, cols], causal[:, at:S],
                                                                 c_tok[:, 1 - q, hh:hh + 1], None, ALU.add)
                                    link(done)
                                dve.wait_ge(s_full, n + 1)
                                if n >= 2:
                                    dve.wait_ge(p_ready, n - 1)
                                for q, cols, at in pieces:
                                    add = (causal_c[:, b, cols] if g == 1
                                           else bias_tab[:, S * hh + at:S * hh + S])
                                    done = dve.tensor_tensor_reduce(
                                        out=logits[:, b, cols], in0=acc[0][:, b, cols], in1=add, scale=1.0,
                                        scalar=-3.0e38, op0=ALU.add, op1=ALU.max,
                                        accum_out=row_max[:, b, q:q + 1])
                                link(done)
                                dve.tensor_scalar(neg_max[:, b, :], row_max[:, b, :], -1.0, None, ALU.mult)\
                                    .then_inc(s_taken, 1)
                            if n in (9, 10):
                                lo_g(g0 + 7, n - 9)
                            if n == HEADS + 1:
                                group_out(0)
                    group_out(1)
                    for h in range(HALVES):
                        xT_low(h, v0)
                    out0, end = g0 + 6, v0 + 2

                if kind == "sgu":
                    def biased(n, c):
                        at = 512 * SGU_ORDER[c]
                        h = [0, 1, 0, 1, 0, 0, 1, 1][n]
                        dve.wait_ge(g_done, 2 * g0 + n + 1)
                        if n >= 2:
                            dve.wait_ge(act_done, a0 + n - 1)
                        dve.tensor_tensor(stage[:, n % 2, :], gu[n % 2][:, :], bias_tab[:, at:at + 512], ALU.add)\
                            .then_inc(gu_taken[n % 2], 1)

                    def gate_y(h):
                        dve.wait_ge(mix_done, h + 1)
                        dve.wait_ge(act_done, a0 + 6 + 2 * h)
                        for g in range(HEADS):
                            cols = slice(P * g, P * g + P)
                            done = dve.scalar_tensor_tensor(
                                out=t_tok[:, h, cols], in0=acc[h][:, g // 4, P * (g % 4):P * (g % 4) + P],
                                scalar=bs_col[:, g:g + 1], in1=u_sgu[:, h, cols], op0=ALU.add, op1=ALU.mult)
                            if g % 4 == 3:
                                done.then_inc(tok_ready, 1)

                    half1()
                    dve.wait_ge(sgu_bias_ld, 16)
                    for n, (c, h) in enumerate([(0, 0), (0, 1), (1, 0), (1, 1)]):
                        lo_g(g0 + c + 1, h)
                        if n == 3:
                            dve.wait_ge(act_done, a0 + 3)
                            ln_stats(v_sgu[:, 0, :], 0)
                        biased(n, c)
                    for j in range(2):
                        ln_apply(v_sgu[:, 0, :], v_sgu[:, 0, :], 0, ln0, j, vn_ready)
                    for part in range(2):
                        lo_g(g0 + 3, part)
                    biased(4, 2)
                    biased(5, 3)
                    gate_y(0)
                    ln_stats(v_sgu[:, 1, :], 1)
                    for j in range(2):
                        ln_apply(v_sgu[:, 1, :], v_sgu[:, 1, :], 1, ln0, j, vn_ready)
                    biased(6, 2)
                    lo_g(g0 + 4, 0)
                    xT_low(0, v0)
                    lo_g(g0 + 4, 1)
                    biased(7, 3)
                    gate_y(1)
                    for part in range(2):
                        lo_g(g0 + 5, part)
                    xT_low(1, v0)
                    ln0, out0, end = ln0 + 1, g0 + 4, v0 + 2

                if kind in ("attn", "sgu"):
                    residual_stats(0, r0, (g_done, 2 * out0 + 2))
                    for j in range(2):
                        x_apply(0, ln0, j)
                    lo_g(out0 + 2, 0)
                    xT_low(0, end)
                    lo_g(out0 + 2, 1)
                    light = False

                    def half1(r0=r0, ln=ln0, done=(g_done, 2 * out0 + 4), use=end):
                        norm_half1(r0, ln, done, use)

        @block.gpsimd
        def _(pool):
            pool.memset(ident[:, :], 0.0).then_inc(pool_step, 1)
            pool.wait_ge(pool_step, 1)
            pool.affine_select(out=ident[:, :], in_=ident[:, :], compare_op=ALU.not_equal, fill=1.0, base=0,
                               pattern=[[-1, P]], channel_multiplier=1).then_inc(const_ready, 1)
            pool.memset(flip[:, :], 0.0).then_inc(pool_step, 1)
            pool.wait_ge(pool_step, 2)
            pool.affine_select(out=flip[:, :], in_=flip[:, :], compare_op=ALU.not_equal, fill=1.0, base=1 - P,
                               pattern=[[1, P]], channel_multiplier=1).then_inc(const_ready, 1)
            pool.dma_start(rel_sb[:, :], rel_bias).then_inc(bias_in, 16)
            pool.dma_start(onehot_sb, bucket_onehot).then_inc(bias_in, 16)
            pool.memset(neg_half, -0.5).then_inc(pool_step, 1)

            def load_ln(ln):
                g, b = [(ln_g[i, s], ln_b[i, s]) for i, s in ((0, 0), (0, 1), (0, 2), (1, 0))][ln] if ln < 4 \
                    else ((sgu_ln_g[0], sgu_ln_b[0]), (ln_g[1, 1], ln_b[1, 1]), (ln_g[1, 2], ln_b[1, 2]))[ln - 4]
                for dst, src in ((gamma, g), (beta, b)):
                    pool.dma_start(dst[:, :], src.partition_broadcast(P)).then_inc(ln_loaded, 16)

            pool.wait_ge(split_a, 2)
            load_ln(0)
            with nc.allow_non_contiguous_dma(reason="eight columns, once"):
                pool.dma_start(wf_raw[:, :, :], attn_w_in[0].rearrange("(b p) n -> p b n", p=P)
                               [:, :, 6 * 512:6 * 512 + HEADS]).then_inc(f_loaded, 16)
                pool.dma_start(bs_col, sgu_b_s[0].rearrange("g t -> t g")).then_inc(rows_loaded, 16)
            pool.dma_start(bf_row, attn_b_f[0].partition_broadcast(P)).then_inc(rows_loaded, 16)
            pool.dma_start(p_tok[:, :, :], p_in[0, 0].rearrange("(h p) n -> p h n", p=P)).then_inc(p_loaded, 16)
            pool.memset(causal[:, :], 0.0).then_inc(pool_step, 1)
            pool.memset(sel[:, :], 0.0).then_inc(pool_step, 1)
            pool.wait_ge(pool_step, 5)
            pool.affine_select(out=causal[:, :], in_=causal[:, :], compare_op=ALU.is_ge, fill=NEG, base=P,
                               pattern=[[-1, S]], channel_multiplier=1).then_inc(const_ready, 1)
            sel_v = sel[:, :].rearrange("p (n t) -> p n t", t=P)
            pool.affine_select(out=sel_v, in_=sel_v, compare_op=ALU.not_equal, fill=1.0, base=0,
                               pattern=[[-1, HEADS], [0, P]], channel_multiplier=1).then_inc(const_ready, 1)
            pool.wait_ge(bias_sb, 1)
            pool.dma_start(bias_rows, bias_row_sb).then_inc(bias_st, 16)
            pool.wait_ge(bias_st, 16)
            ln_end = []
            for k, (kind, _, _) in enumerate(PHASES):
                if kind == "ffn":
                    ln_end.append((tok_ready, bases[k]["x"] + 4))
                elif kind == "sgu":
                    ln_end.append((vn_ready, 4))
                if kind in ("attn", "sgu"):
                    ln_end.append((tok_ready, bases[k]["x"] + 8))
            for ln in range(total["ln"]):
                for h in range(HALVES):
                    pool.wait_ge(var_ready, 2 * ln + h + 1)
                    pool.tensor_tensor(rstd[:, h:h + 1], var_eps[:, h:h + 1], neg_half, ALU.pow)\
                        .then_inc(rstd_ready, 1)
                if ln == 0:
                    pool.wait_ge(d_done, 2 * NCH)
                    pool.dma_start(bias_rev[:, :, :].rearrange("p h (n u) -> p (h n) u", u=S),
                                   bass.AP(bias_rows.tensor, 0, [[1, P], [512, HEADS], [1, S]]))\
                        .then_inc(bias_ld, 16)
                if ln == 2:
                    pool.dma_start(bias_tab[:, :], sgu_b_in[0].partition_broadcast(P)).then_inc(sgu_bias_ld, 16)
                if ln == 3:
                    pool.dma_start(ws_tok[:, :, :], sgu_w_s[0].rearrange("g t s -> t g s"))\
                        .then_inc(ws_raw, 16)
                    pool.wait_ge(ws_raw, 16)
                    pool.affine_select(out=ws_tok[:, :, :], in_=ws_tok[:, :, :], compare_op=ALU.is_ge, fill=0.0,
                                       base=0, pattern=[[0, HEADS], [-1, P]], channel_multiplier=1)\
                        .then_inc(ws_loaded, 1)
                    pool.dma_start(p_tok[:, :, :], p_in[1, 0].rearrange("(h p) n -> p h n", p=P))\
                        .then_inc(p_loaded, 16)
                if ln + 1 < total["ln"]:
                    pool.wait_ge(*ln_end[ln])
                    load_ln(ln + 1)


def bucket_of(n):
    exact = BUCKETS // 2
    if n < exact:
        return n
    big = exact + int(np.float32(np.log(np.float32(n / exact))) / np.float32(math.log(128 / exact))
                      * np.float32(BUCKETS - exact))
    return min(big, BUCKETS - 1)


_INS = ["x", "p", "ln_g", "ln_b", "ffn_w_gate", "ffn_w_up", "ffn_w_down", "attn_w_in", "attn_b_f", "attn_w_out",
        "rel_bias", "sgu_w_in", "sgu_b_in", "sgu_ln_g", "sgu_ln_b", "sgu_w_s", "sgu_b_s", "sgu_w_out",
        "ple_w_proj", "ple_w_gate"]


def kernel(**inputs):
    import concourse.bacc as bacc
    from concourse.bass_utils import run_bass_kernel_spmd

    nc = bacc.Bacc("TRN2", target_bir_lowering=False, num_devices=1)
    onehot = np.zeros((BUCKETS, 512), np.float32)
    for j in range(S):
        onehot[bucket_of(S - 1 - j), j] = 1.0
    arrays = {"in_bucket_onehot": onehot}
    args = [nc.dram_tensor("in_bucket_onehot", onehot.shape, F32, kind="ExternalInput").ap()]
    for name in _INS:
        a = np.ascontiguousarray(inputs[name])
        arrays[f"in_{name}"] = a
        args.append(nc.dram_tensor(f"in_{name}", a.shape, mybir.dt.from_np(a.dtype), kind="ExternalInput").ap())
    out = nc.dram_tensor("out_0", (1, S, D), F32, kind="ExternalOutput").ap()
    build(nc, *args, out)
    r = run_bass_kernel_spmd(nc, [arrays], core_ids=[0])
    return r.results[0]["out_0"]
```

```python
import math
from contextlib import ExitStack

import numpy as np

import concourse.bass as bass
from concourse import mybir

F32 = mybir.dt.float32
F32R = mybir.dt.float32r
ALU = mybir.AluOpType
ACT = mybir.ActivationFunctionType
AXX = mybir.AxisListType.X

P = 128
D = 1024
S = 256
HALVES = S // P
KB = D // P
FF = 2816
FC = 256
NCH = FF // FC
HD = 64
HEADS = 8
PLE = 256
DEPTH = 2
ALPHA = (2.0 * DEPTH) ** 0.25
EPS = 1e-5
WARM = 7
NEG = -1e30
SCALE = HD ** -0.5
BUCKETS = 32
PHASES = [("ffn", 0, 0), ("attn", 0, 1), ("ffn", 0, 2), ("ple", 0, 0),
          ("ffn", 1, 0), ("sgu", 1, 1), ("ffn", 1, 2), ("ple", 1, 0)]
SGU_ORDER = [2, 3, 0, 1]


PAIR = [(0, 0), (1, 0), (0, 1), (1, 1)]
ATTN_ORDER = [
    ("g", 0, 0), ("half1",), ("flip",), ("g", 0, 1), ("turn", 0, 0), ("forget",),
    ("g", 1, 0), ("turn", 0, 1), ("exp",), ("g", 1, 1), ("turn", 1, 0), ("log",),
    ("g", 2, 0), ("turn", 1, 1), ("g", 2, 1), ("cT",),
    ("g", 3, 0), ("head", 0), ("g", 3, 1), ("turn", 3, 0), ("head", 1),
    ("g", 4, 0), ("turn", 3, 1), ("head", 2), ("g", 4, 1), ("turn", 4, 0), ("head", 3), ("head", 4),
    ("g", 5, 0), ("turn", 4, 1), ("head", 5), ("head", 6), ("g", 5, 1), ("head", 7), ("head", 8),
] + [("head", n) for n in range(HEADS + 1, 2 * HEADS + 2)] + [("oT", 0), ("oT", 1)]


def attn_tp_uses():
    uses, count = {}, [0, 0]
    for e in ATTN_ORDER:
        if e[0] == "turn":
            banks = [(e, e[2])]
        elif e[0] == "oT":
            banks = [(e, 1 - e[1])]
        elif e[0] == "cT":
            banks = [(("cT", h), h) for h in range(HALVES)]
        elif e[0] == "head" and e[1] >= 1 and e[1] <= 2 * HEADS:
            banks = [(("probs", e[1] - 1), (e[1] - 1) % 2)]
        else:
            banks = []
        for key, bank in banks:
            uses[key] = (bank, count[bank])
            count[bank] += 1
    return uses


def p_use(s, c, h):
    return 1 if s == 2 and c >= 2 - h else 0


def phase_bases():
    per = {"ffn": dict(g=NCH, d=NCH, u=NCH, t=NCH + 2, v=NCH + 2, a=2 * NCH, x=4, r=4, ln=1),
           "attn": dict(g=8, d=0, u=6, t=5 + HEADS + 1 + 2, v=3, a=0, x=8, r=4, ln=1),
           "sgu": dict(g=6, d=0, u=4, t=2 + 2, v=4, a=8, x=8, r=4, ln=2),
           "ple": dict(g=2, d=1, u=2, t=2, v=2, a=4, x=4, r=0, ln=0)}
    now = dict(g=0, d=0, u=0, t=2, v=2, a=0, x=0, r=0, ln=0)
    out = []
    for kind, _, s in PHASES:
        out.append(dict(now))
        now = {k: now[k] + per[kind][k] for k in now}
        if kind == "ffn" and s == 2:
            now["t"] += 1
            now["v"] += 1
    return out, now


def build(nc, bucket_onehot, x_in, p_in, ln_g, ln_b, w_gate, w_up, w_down, attn_w_in, attn_b_f, attn_w_out,
          rel_bias, sgu_w_in, sgu_b_in, sgu_ln_g, sgu_ln_b, sgu_w_s, sgu_b_s, sgu_w_out, ple_w_proj,
          ple_w_gate, out):
    bases, total = phase_bases()
    tp_of = attn_tp_uses()
    pair_firsts = set()
    for k, (kind, _, _) in enumerate(PHASES):
        pair_firsts |= {bases[k]["g"] + q for q in {"ffn": (), "attn": (6,), "sgu": (4,), "ple": (0,)}[kind]}

    def g_used(m):
        return 2 * m + 3 if isinstance(m, int) and m in pair_firsts else 2 * m + 2

    bias_rows = nc.dram_tensor("bias_rows", (HEADS, 512), F32, kind="Internal").ap()

    with ExitStack() as ctx:
        def sb(name, shape, dt=F32, where=ctx):
            return where.enter_context(nc.sbuf_tensor(name, shape, dt))

        def sem(name):
            return ctx.enter_context(nc.semaphore(name))

        rawA = sb("rawA", [P, 4, 512])
        rawB = sb("rawB", [P, 4, 512])
        rawD = sb("rawD", [P, 2, D])
        g_hi = sb("g_hi", [P, 2, KB, 512], F32R)
        g_lo = sb("g_lo", [P, 2, KB, 512], F32R)
        x_tok = sb("x_tok", [P, HALVES, D])
        t_tok = sb("t_tok", [P, HALVES, D])
        xT_hi = sb("xT_hi", [P, KB, S], F32R)
        xT_lo = sb("xT_lo", [P, KB, S], F32R)
        stage = sb("stage", [P, HALVES, 512])
        hT_hi = sb("hT_hi", [P, 3, 2, P], F32R)
        hT_lo = sb("hT_lo", [P, 3, 2, P], F32R)
        pT_hi = sb("pT_hi", [P, HALVES, 2, P], F32R)
        pT_lo = sb("pT_lo", [P, HALVES, 2, P], F32R)
        gamma = sb("gamma", [P, D])
        beta = sb("beta", [P, D])
        bias_tab = sb("bias_tab", [P, 2048])
        p_tok = sb("p_tok", [P, HALVES, PLE])
        probs = sb("probs", [P, 2, 384])
        logits = sb("logits", [P, 2, 384])
        probsT = sb("probsT", [P, 2, 384])
        ident = sb("ident", [P, P])
        flip = sb("flip", [P, P])
        wf_raw = sb("wf_raw", [P, KB, HEADS])
        wf_hi = sb("wf_hi", [P, KB, HEADS], F32R)
        wf_lo = sb("wf_lo", [P, KB, HEADS], F32R)
        small = sb("small", [P, 256])
        c_tok = small[:, 16:32].rearrange("p (h n) -> p h n", h=2)
        bf_col = small[0:HEADS, 32:33]
        row_sum = small[:, 40:72].rearrange("p (i n) -> p i n", i=2)
        row_inv = small[:, 72:104].rearrange("p (i n) -> p i n", i=2)
        row_max = small[:, 104:108].rearrange("p (b i) -> p b i", b=2)
        neg_max = small[:, 108:112].rearrange("p (b i) -> p b i", b=2)
        stats = small[:, 112:136].rearrange("p (h n) -> p h n", h=2)
        mean_var = small[:, 136:140].rearrange("p (h n) -> p h n", h=2)
        var_eps = small[:, 140:142]
        rstd = small[:, 142:144]
        neg_half = small[:, 144:145]
        bs_col = small[:, 152:160]
        with ExitStack() as region:
            d_hi = sb("d_hi", [P, 2, 2, D], F32R, region)
            d_lo = sb("d_lo", [P, 2, 2, D], F32R, region)
        with ExitStack() as region:
            qT = sb("qT", [P, HEADS, S], where=region)
            kT = sb("kT", [P, HEADS, S], where=region)
            v_att = sb("v_att", [P, HALVES, 2 * 512], where=region)
            head_c = sb("head_c", [HEADS, 2048], where=region)
        bias_rev = v_att
        with ExitStack() as region:
            u_sgu = sb("u_sgu", [P, HALVES, D], where=region)
            v_sgu = sb("v_sgu", [P, HALVES, D], where=region)
            ws_tok = sb("ws_tok", [P, HEADS, P], where=region)
            ws_T = sb("ws_T", [P, HEADS, P], where=region)
        region_end = sb("region_tail", [P, 2, 2 * D + 2 * D])
        del region_end
        causal = sb("causal", [P, S])
        causal_c = sb("causal_c", [P, 2, 384])
        rel_sb = sb("rel_sb", [BUCKETS, HEADS])
        onehot_sb = probs[0:BUCKETS, :, :].rearrange("p a b -> p (a b)")[:, 0:512]
        bias_row_sb = logits[0:HEADS, :, :].rearrange("p a b -> p (a b)")[:, 0:512]
        c_hi = sb("c_hi", [HEADS, S + P], F32R)
        c_lo = sb("c_lo", [HEADS, S + P], F32R)
        sel_r = sb("sel_r", [HEADS, HEADS * P], F32R)
        lf = head_c[:, :].rearrange("p (n s) -> p n s", s=S)

        acc = [ctx.enter_context(nc.psum_tensor(f"acc{h}", [P, 2, 512], F32)) for h in range(2)]
        gu = [ctx.enter_context(nc.psum_tensor(f"gu{h}", [P, 512], F32)) for h in range(2)]
        tp = [ctx.enter_context(nc.psum_tensor(f"tp{h}", [P, 512], F32)) for h in range(2)]

        heads_out = [[acc[1][:, 0, :], acc[1][:, 1, :]], [gu[0][:, :], gu[1][:, :]]]

        raw_a, raw_b, raw_d = sem("raw_a"), sem("raw_b"), sem("raw_d")
        high_a, high_b, high_d = sem("high_a"), sem("high_b"), sem("high_d")
        raw_q, high_q, split_q = sem("raw_q"), sem("high_q"), sem("split_q")
        split_a, split_b, split_d = sem("split_a"), sem("split_b"), sem("split_d")
        g_done = sem("g_done")
        d_first = sem("d_first")
        d_done = sem("d_done")
        gu_taken = [sem("gu_taken0"), sem("gu_taken1")]
        tp_full = [sem("tp_full0"), sem("tp_full1")]
        tp_hi = [sem("tp_hi0"), sem("tp_hi1")]
        tp_taken = [sem("tp_taken0"), sem("tp_taken1")]
        act_done = sem("act_done")
        tok_ready = sem("tok_ready")
        acc_read = sem("acc_read")
        x_loaded, p_loaded = [sem("x_loaded0"), sem("x_loaded1")], sem("p_loaded")
        ln_loaded = sem("ln_loaded")
        var_ready, rstd_ready = sem("var_ready"), sem("rstd_ready")
        step = sem("step")
        const_ready, pool_step = sem("const_ready"), sem("pool_step")
        bias_in, bias_mm, bias_sb, bias_st, bias_ld, bias_flip, bias_done = (
            sem("bias_in"), sem("bias_mm"), sem("bias_sb"), sem("bias_st"), sem("bias_ld"), sem("bias_flip"),
            sem("bias_done"))
        f_loaded, f_hi, f_split, f_mm, f_exp, f_arg, f_ln, f_cum = (
            sem("f_loaded"), sem("f_hi"), sem("f_split"), sem("f_mm"), sem("f_exp"),
            sem("f_arg"), sem("f_ln"), sem("f_cum"))
        s_full, s_taken, p_ready, pv_done = sem("s_full"), sem("s_taken"), sem("p_ready"), sem("pv_done")
        o_turned, o_hi, o_split = sem("o_turned"), sem("o_hi"), sem("o_split")
        ws_loaded, vn_ready, mix_done, sgu_bias_ld, ws_raw = (
            sem("ws_loaded"), sem("vn_ready"), sem("mix_done"), sem("sgu_bias_ld"),
            sem("ws_raw"))
        ws_turned, ws_taken = sem("ws_turned"), sem("ws_taken")
        rows_loaded = sem("rows_loaded")
        out_done = sem("out_done")

        block = ctx.enter_context(nc.Block())

        def g_source(k, c, part):
            kind, i, s = PHASES[k]
            rows = slice(4 * part, 4 * part + 4)
            if kind == "ffn":
                cols = bass.DynSlice(c * FC, FC)
                gate = w_gate[i, s // 2].rearrange("(b p) n -> p b n", p=P)[:, rows, cols]
                up = w_up[i, s // 2].rearrange("(b p) n -> p b n", p=P)[:, rows, cols]
                return [(slice(0, 4), slice(0, FC), gate), (slice(0, 4), slice(FC, 2 * FC), up)]
            if kind == "attn":
                w, c = (attn_w_in[0], c) if c < 6 else (attn_w_out[0], c - 6)
            elif kind == "sgu":
                w, c = (sgu_w_in[0], SGU_ORDER[c]) if c < 4 else (sgu_w_out[0], c - 4)
            else:
                w = ple_w_gate[i]
            v = w.rearrange("(b p) n -> p b n", p=P)[:, rows, 512 * c:512 * c + 512]
            return [(slice(0, 2), slice(0, 512), v[:, 0:2]), (slice(2, 4), slice(0, 512), v[:, 2:4])]

        @block.sync
        def _(sp):
            def load_half(n, k, c, part):
                raw, loaded, split = ((rawA, raw_a, split_a), (rawB, raw_b, split_b))[part]
                if not (isinstance(n, int) and n == 0):
                    sp.wait_ge(split, n)
                for b, cols, src in g_source(k, c, part):
                    sp.dma_start(raw[:, b, cols], src).then_inc(loaded, 16)

            def load_d(m, src):
                if not (isinstance(m, int) and m == 0):
                    sp.wait_ge(split_d, m)
                sp.dma_start(rawD[:, :, :], src).then_inc(raw_d, 16)

            def load_x(h):
                sp.dma_start(x_tok[:, h, :], x_in[0, h * P:(h + 1) * P, :]).then_inc(x_loaded[h], 16)

            load_x(0)
            for loaded, ks in ((raw_q, slice(0, 2)), (raw_a, slice(2, 4))):
                for b, cols, src in g_source(0, 0, 0):
                    sp.dma_start(rawA[:, ks, cols], src[:, ks]).then_inc(loaded, 16)
            load_half(0, 0, 0, 1)
            load_x(1)
            for k, (kind, i, s) in enumerate(PHASES):
                g0, d0 = bases[k]["g"], bases[k]["d"]
                chunks = {"ffn": NCH, "attn": 8, "sgu": 6, "ple": 2}[kind]

                def load_next(c, part):
                    if c + 1 < chunks:
                        load_half(g0 + c + 1, k, c + 1, part)
                    elif k + 1 < len(PHASES):
                        load_half(g0 + c + 1, k + 1, 0, part)

                if kind == "ffn":
                    down = w_down[i, s // 2].rearrange("(c b p) n -> p c b n", b=2, p=P)
                    load_next(0, 0)
                    load_d(d0, down[:, 0])
                    load_next(0, 1)
                    with sp.Fori(1, NCH - 1) as c:
                        load_half(g0 + 1 + c, k, c + 1, 0)
                        load_d(d0 + c, down[:, bass.DynSlice(c, 1)])
                        load_half(g0 + 1 + c, k, c + 1, 1)
                    load_next(NCH - 1, 0)
                    load_d(d0 + NCH - 1, down[:, NCH - 1])
                    load_next(NCH - 1, 1)
                    if s == 2:
                        load_d(d0 + NCH, ple_w_proj[i].rearrange("(b p) n -> p b n", p=P))
                else:
                    for c in range(chunks):
                        for part in range(2):
                            load_next(c, part)
            for n, (j, h) in enumerate(PAIR):
                sp.wait_ge(tok_ready, bases[-1]["x"] + n + 1)
                sp.dma_start(out[0, h * P:(h + 1) * P, 512 * j:512 * j + 512],
                             x_tok[:, h, 512 * j:512 * j + 512]).then_inc(out_done, 16)
            sp.wait_ge(out_done, 4 * 16)

        @block.tensor
        def _(pe):
            def product(dst, hi, lo, w_hi, w_lo, first=True, last=True):
                for b in range(len(hi)):
                    pe.matmul(dst, hi[b], w_hi[b], start=first and b == 0, stop=False)
                    pe.matmul(dst, hi[b], w_lo[b], start=False, stop=False)
                    done = pe.matmul(dst, lo[b], w_hi[b], start=False, stop=last and b == len(hi) - 1)
                return done

            def g_piece(slot, h, dst, k_from, k_to):
                tok = slice(h * P, (h + 1) * P)
                ks = range(k_from, k_to)
                return product(dst, [xT_hi[:, b, tok] for b in ks], [xT_lo[:, b, tok] for b in ks],
                               [g_hi[:, slot, b, :] for b in ks], [g_lo[:, slot, b, :] for b in ks],
                               first=k_from == 0, last=k_to == KB)

            def g_product(n, slot, h, dst, operand_wait=None, between=None, parts=(0, 1)):
                first = isinstance(n, int) and n == 0 and h == 0
                for part in parts:
                    if operand_wait is not None:
                        operand_wait(part, h)
                    if first and part == 0:
                        pe.wait_ge(split_q, 1)
                        g_piece(slot, h, dst, 0, 2)
                    if h == 0:
                        pe.wait_ge((split_a, split_b)[part], n + 1)
                    done = g_piece(slot, h, dst, 2 if first and part == 0 else 4 * part, 4 * part + 4)
                    if part == 0 and between is not None:
                        between()
                done.then_inc(g_done, 1)

            def bank_free(bank, uses):
                if not (isinstance(uses, int) and uses == 0):
                    pe.wait_ge(gu_taken[bank], uses)

            def d_product(m, slot, h, hi, lo, first, last, js=(0, 1)):
                pe.wait_ge(split_d, m + 1)
                for j in js:
                    cols = slice(512 * j, 512 * j + 512)
                    done = product(acc[h][:, j, :], [hi[:, b, :] for b in range(2)],
                                   [lo[:, b, :] for b in range(2)],
                                   [d_hi[:, slot, b, cols] for b in range(2)],
                                   [d_lo[:, slot, b, cols] for b in range(2)], first=first, last=last)
                    if j == 0 and last:
                        done.then_inc(d_first, 1)
                if 1 in js:
                    done.then_inc(d_done, 1)

            def transposes(bank, use, srcs):
                if not (isinstance(use, int) and use == 0):
                    pe.wait_ge(tp_taken[bank], use)
                for q, src in enumerate(srcs):
                    rows = src.shape[0]
                    done = pe.transpose(tp[bank][0:src.shape[1], rows * q:rows * q + rows], src,
                                        ident[0:rows, 0:rows])
                done.then_inc(tp_full[bank], 1)

            def token_transposes(src, h, use, needs):
                for j in range(2):
                    pe.wait_ge(*needs[j])
                    transposes(j, use, [src[:, h, 512 * j + P * q:512 * j + P * q + P] for q in range(4)])

            def xT_wait(h, use):
                for j in range(2):
                    pe.wait_ge(tp_taken[j], use[h] + 1)

            def ln_turn(h, x0, use):
                token_transposes(x_tok, h, use[h], [(tok_ready, x0 + 2 * h + j + 1) for j in range(2)])

            pe.wait_ge(const_ready, 1)
            use = (0, 1)
            token_transposes(x_tok, 0, 0, [(x_loaded[0], 16)] * 2)
            for _ in range(WARM):
                pe.matmul(acc[0][:, 0, 0:P], ident[:, :], ident[:, :], start=True, stop=True)

            def half1():
                token_transposes(x_tok, 1, 1, [(x_loaded[1], 16)] * 2)

            for k, (kind, i, s) in enumerate(PHASES):
                B = bases[k]
                g0, d0, u0, t0, x0, a0 = (B[q] for q in ("g", "d", "u", "t", "x", "a"))

                if kind == "ffn":
                    def up(c, cs, h, between=None):
                        bank_free(h, u0 + c)
                        g_product(g0 + c, (g0 + cs) % 2, h, gu[h][:, :], between=between)

                    def turn(c, cs, h):
                        pe.wait_ge(gu_taken[h], u0 + c + 1)
                        transposes(h, t0 + c + p_use(s, cs, h), [stage[:, h, FC + P * b:FC + P * b + P] for b in range(2)])

                    def down(c, cs, h, js=(0, 1)):
                        pe.wait_ge(tp_taken[h], t0 + c + (2 if s == 2 and cs >= 1 else 1))
                        if k == 0 and cs == 0 and h == 1:
                            pe.wait_ge(bias_sb, 1)
                        at = 2 if h == 1 and cs == NCH - 1 else h
                        d_product(d0 + c, (d0 + cs) % 2, h, hT_hi[:, at], hT_lo[:, at], first=cs == 0,
                                  last=cs == NCH - 1, js=js)

                    def chunk(c, cs):
                        up(c, cs, 0)
                        turn(c - 1, cs - 1, 1)
                        down(c - 1, cs - 1, 0)
                        up(c, cs, 1)
                        turn(c, cs, 0)
                        down(c - 1, cs - 1, 1)

                    xT_wait(0, use)
                    if k == 0 or PHASES[k - 1][0] == "ple":
                        up(0, 0, 0, between=half1)
                    else:
                        up(0, 0, 0)
                        half1()
                    xT_wait(1, use)
                    up(0, 0, 1)
                    if k == 0:
                        pe.wait_ge(bias_in, 32)
                        pe.matmul(acc[1][0:HEADS, 1, :], rel_sb[:, :], onehot_sb, start=True,
                                  stop=True).then_inc(bias_mm, 1)
                    turn(0, 0, 0)
                    chunk(1, 1)
                    if s == 2:
                        pe.wait_ge(p_loaded, 16 * (i + 1))
                        for h in range(HALVES):
                            transposes(h, t0 + 2 - h, [p_tok[:, h, P * b:P * b + P] for b in range(2)])
                    with pe.Fori(0, (NCH - 3) // 2) as r:
                        for e in range(2):
                            chunk(r * 2 + (2 + e), 2 + e)
                    c = NCH - 1
                    up(c, c, 0)
                    turn(c - 1, c - 1, 1)
                    down(c - 1, c - 1, 0)
                    turn(c, c, 0)
                    bank_free(1, u0 + c)
                    g_piece((g0 + c) % 2, 1, gu[1][:, :], 0, 2)
                    down(c, c, 0)
                    g_piece((g0 + c) % 2, 1, gu[1][:, :], 2, KB).then_inc(g_done, 1)
                    down(c - 1, c - 1, 1, (0,))
                    turn(c, c, 1)
                    down(c - 1, c - 1, 1, (1,))
                    use = (t0 + NCH + p_use(s, c, 0), t0 + NCH + p_use(s, c, 1) + 1)
                    ln_turn(0, x0, use)
                    down(c, c, 1)

                    def half1(x0=x0, use=use):
                        ln_turn(1, x0, use)

                if kind == "ple":
                    for n, (j, h) in enumerate(PAIR):
                        if n < 2:
                            bank_free(j, u0)
                        else:
                            pe.wait_ge(act_done, a0 + n - 1)
                        if n % 2 == 0:
                            xT_wait(h, use)
                        if n == 3 and k + 1 < len(PHASES):
                            ln_turn(0, x0, (t0, t0 + 1))
                        g_product(g0 + j, (g0 + j) % 2, h, gu[j][:, :])
                        if n == 1:
                            half1()
                            d_product(d0, d0 % 2, 0, pT_hi[:, 0], pT_lo[:, 0], first=True, last=True)
                        if n == 2:
                            d_product(d0, d0 % 2, 1, pT_hi[:, 1], pT_lo[:, 1], first=True, last=True)
                    use = (t0, t0 + 1)

                    def half1(x0=x0, use=use):
                        ln_turn(1, x0, use)

                if kind == "attn":
                    def scores(n):
                        g, hh, sl = n // HEADS, n % HEADS, n % 2
                        rows, blk = slice(HD * (hh % 2), HD * (hh % 2) + HD), 4 * g + hh // 2
                        if n == 0:
                            pe.wait_ge(f_arg, 1)
                        if hh == 0:
                            for b in range(2):
                                pe.wait_ge(tp_taken[b], t0 + tp_of[("turn", 3 * g + 1, b)][1] + 1)
                        if n >= 2:
                            pe.wait_ge(s_taken, n - 1)
                        if n == HEADS:
                            pe.wait_ge(const_ready, 4)
                        if g == 1:
                            for start, c_part in ((True, c_hi), (False, c_lo)):
                                pe.matmul(acc[0][:, sl, 0:S + P], sel_r[:, hh * P:hh * P + P], c_part[:, :],
                                          start=start, stop=False)
                        for i_q, cols in ((1, slice(0, S)), (0, slice(S, S + P))):
                            done = pe.matmul(acc[0][:, sl, cols], qT[rows, blk, i_q * P:i_q * P + P],
                                             kT[rows, blk, 0:cols.stop - cols.start], start=g == 0,
                                             stop=g == 0 or i_q == 0)
                        done.then_inc(s_full, 1)

                    def probs_turn(n):
                        pe.wait_ge(p_ready, n + 1)
                        bank, at = tp_of[("probs", n)]
                        transposes(bank, t0 + at, [probs[:, bank, P * q:P * q + P] for q in range(3)])

                    def values(n):
                        g, hh, sl = n // HEADS, n % HEADS, n % 2
                        pe.wait_ge(tp_taken[sl], t0 + tp_of[("probs", n)][1] + 1)
                        if hh == 0:
                            for h in range(HALVES):
                                pe.wait_ge(gu_taken[h], u0 + 3 * (g + 1))
                        vc = slice(g * 512 + hh * HD, g * 512 + hh * HD + HD)
                        oc = slice(hh * HD, hh * HD + HD)
                        o = heads_out[g]
                        pe.matmul(o[0][:, oc], probsT[:, sl, 2 * P:3 * P], v_att[:, 0, vc],
                                  start=True, stop=True)
                        pe.matmul(o[1][:, oc], probsT[:, sl, 0:P], v_att[:, 0, vc], start=True, stop=False)
                        pe.matmul(o[1][:, oc], probsT[:, sl, P:2 * P], v_att[:, 1, vc],
                                  start=False, stop=True).then_inc(pv_done, 1)

                    for e in ATTN_ORDER:
                        if e[0] == "g":
                            c, h = e[1:]
                            if c == 0:
                                xT_wait(h, use)
                            bank_free(h, u0 + c)
                            g_product(g0 + c, (g0 + c) % 2, h, gu[h][:, :])
                        elif e[0] == "half1":
                            half1()
                        elif e[0] == "turn":
                            c, h = e[1:]
                            pe.wait_ge(gu_taken[h], u0 + c + 1)
                            transposes(h, t0 + tp_of[e][1], [stage[:, h, P * q:P * q + P] for q in range(4)])
                        elif e[0] == "forget":
                            pe.wait_ge(f_split, 1)
                            pe.wait_ge(bias_done, 1)
                            product(acc[0][0:HEADS, 0, 0:S], [wf_hi[:, b, :] for b in range(KB)],
                                    [wf_lo[:, b, :] for b in range(KB)], [xT_hi[:, b, :] for b in range(KB)],
                                    [xT_lo[:, b, :] for b in range(KB)]).then_inc(f_mm, 1)
                        elif e[0] == "flip":
                            pe.wait_ge(bias_ld, 16)
                            for q in range(4):
                                done = pe.matmul(acc[q // 2][:, q % 2, :], flip[:, :],
                                                 bias_rev[:, q // 2, 512 * (q % 2):512 * (q % 2) + 512],
                                                 start=True, stop=True)
                            done.then_inc(bias_flip, 1)
                        elif e[0] == "cT":
                            pe.wait_ge(f_cum, 1)
                            for h in range(HALVES):
                                transposes(h, t0 + tp_of[("cT", h)][1], [lf[:, 0, h * P:(h + 1) * P]])
                        elif e[0] == "head":
                            n = e[1]
                            if n < 2 * HEADS:
                                scores(n)
                            if n in (13, 14):
                                h = n - 13
                                pe.wait_ge(tok_ready, x0 + h + 1)
                                for q in range(4):
                                    done = pe.transpose(acc[1][:, h, P * q:P * q + P],
                                                        t_tok[:, h, P * q:P * q + P], ident[:, :])
                                done.then_inc(o_turned, 1)
                            if 1 <= n <= 2 * HEADS:
                                probs_turn(n - 1)
                            if n >= 2:
                                values(n - 2)
                    out0, y_turn = g0 + 6, None
                    after = (t0 + 5 + HEADS + 1, t0 + 5 + HEADS + 2)

                    def y_wait(j, h):
                        if j == 0:
                            pe.wait_ge(o_split, h + 1)
                        else:
                            bank, at = tp_of[("oT", h)]
                            pe.wait_ge(tp_taken[bank], t0 + at + 1)

                    def y_rest():
                        for h in range(HALVES):
                            bank, at = tp_of[("oT", h)]
                            pe.wait_ge(tok_ready, x0 + 2 + h + 1)
                            transposes(bank, t0 + at,
                                       [t_tok[:, h, 512 + P * q:512 + P * q + P] for q in range(4)])
                        y_wait(0, 1)
                        g_piece((g0 + 6) % 2, 1, acc[1][:, 0, :], 0, 4)

                if kind == "sgu":
                    def mix(h):
                        pe.wait_ge(vn_ready, 2 * (h + 1))
                        for g in range(HEADS):
                            done = pe.matmul(acc[h][:, g // 4, P * (g % 4):P * (g % 4) + P], ws_T[:, g, :],
                                             v_sgu[:, h, P * g:P * g + P], start=True, stop=True)
                        done.then_inc(mix_done, 1)

                    def y_turn(h):
                        token_transposes(t_tok, h, t0 + h, [(tok_ready, x0 + 2 * h + j + 1) for j in range(2)])

                    for n, (c, h) in enumerate((c, h) for c in range(4) for h in range(2)):
                        if c == 0:
                            xT_wait(h, use)
                        bank_free(n % 2, u0 + n // 2)
                        g_product(g0 + c, (g0 + c) % 2, h, gu[n % 2][:, :])
                        if n == 0:
                            half1()
                            pe.wait_ge(ws_loaded, 1)
                            for g in range(HEADS):
                                done = pe.transpose(acc[0][:, g // 4, P * (g % 4):P * (g % 4) + P],
                                                    ws_tok[:, g, :], ident[:, :])
                            done.then_inc(ws_turned, 1)
                        if n == 5:
                            pe.wait_ge(ws_taken, 1)
                            mix(0)
                        if n == 7:
                            y_turn(0)
                            mix(1)
                    use, out0, after = (t0, t0 + 1), g0 + 4, (t0 + 2, t0 + 3)

                    y_rest = None

                    def y_wait(j, h, use=use):
                        pe.wait_ge(tp_taken[j], use[h] + 1)

                if kind in ("attn", "sgu"):
                    for n, (j, h) in enumerate(PAIR):
                        if n == 2 and y_turn is not None:
                            y_turn(1)
                        if n == 3:
                            ln_turn(0, x0 + 4, after)
                        g_product(out0 + j, (out0 + j) % 2, h, acc[h][:, j, :],
                                  y_wait if n % 2 == 0 else None, y_rest if n == 0 else None,
                                  (1,) if n == 2 and y_rest is not None else (0, 1))
                    use = after

                    def half1(x0=x0 + 4, use=use):
                        ln_turn(1, x0, use)

        @block.scalar
        def _(act):
            def copy(dst, src, scale=1.0):
                return act.activation(dst, src, ACT.Copy, scale=scale)

            def hi_g(n, part):
                raw, loaded, done = ((rawA, raw_a, high_a), (rawB, raw_b, high_b))[part]
                hi_g_into(n, n % 2, part)

            def hi_g_into(n, slot, part):
                raw, loaded, done = ((rawA, raw_a, high_a), (rawB, raw_b, high_b))[part]
                act.wait_ge(loaded, 32 * n + 32)
                if not (isinstance(n, int) and n < 2):
                    act.wait_ge(g_done, g_used(n - 2))
                copy(g_hi[:, slot, 4 * part:4 * part + 4, :], raw[:, :, :]).then_inc(done, 1)

            def hi_d(m, slot, free=None):
                act.wait_ge(raw_d, 16 * m + 16)
                if not (isinstance(m, int) and m < 2):
                    act.wait_ge(d_done, 2 * m - 2 if free is None else free)
                copy(d_hi[:, slot, :, :], rawD[:, :, :]).then_inc(high_d, 1)

            def xT_high(h, use):
                for j in range(2):
                    xT_high_block(j, h, use + h, bank=j)

            def xT_high_block(j, h, use, bank):
                act.wait_ge(tp_full[bank], use + 1)
                copy(xT_hi[:, 4 * j:4 * j + 4, h * P:(h + 1) * P],
                     tp[bank][:, :].rearrange("p (b t) -> p b t", b=4)).then_inc(tp_hi[bank], 1)

            def hT_high(h, use, at=None):
                act.wait_ge(tp_full[h], use + 1)
                copy(hT_hi[:, h if at is None else at, :, :], tp[h][:, 0:2 * P].rearrange("p (b t) -> p b t", b=2)).then_inc(tp_hi[h], 1)

            xT_high(0, 0)
            act.wait_ge(raw_q, 32)
            copy(g_hi[:, 0, 0:2, :], rawA[:, 0:2, :]).then_inc(high_q, 1)
            act.wait_ge(raw_a, 32)
            copy(g_hi[:, 0, 2:4, :], rawA[:, 2:4, :]).then_inc(high_a, 1)
            hi_g(0, 1)

            def half1():
                xT_high(1, 0)

            for k, (kind, i, s) in enumerate(PHASES):
                B = bases[k]
                g0, d0, u0, t0, x0, a0 = (B[q] for q in ("g", "d", "u", "t", "x", "a"))
                last_phase = k + 1 == len(PHASES)

                if kind == "ffn":
                    def gate(c, h, value=None):
                        act.wait_ge(g_done, 2 * c + (2 * g0 + h + 1))
                        act.activation(stage[:, h, 0:FC], gu[h][:, 0:FC], ACT.Silu).then_inc(act_done, 1)

                    def chunk(c, cs):
                        slot = (g0 + cs + 1) % 2
                        if k == 0 and cs == 0:
                            half1()
                        hi_g_into(c + (g0 + 1), slot, 0)
                        if k > 0 and cs == 0:
                            half1()
                        gate(c, 0)
                        if cs > 0:
                            hT_high(1, c + (t0 - 1 + p_use(s, cs - 1, 1)))
                        hi_d(c + d0, (d0 + cs) % 2)
                        hi_g_into(c + (g0 + 1), slot, 1)
                        gate(c, 1)
                        hT_high(0, c + (t0 + p_use(s, cs, 0)))

                    chunk(0, 0)
                    chunk(1, 1)
                    if s == 2:
                        for h in range(HALVES):
                            act.wait_ge(tp_full[h], t0 + 3 - h)
                            copy(pT_hi[:, h, :, :], tp[h][:, 0:2 * P].rearrange("p (b t) -> p b t", b=2))\
                                .then_inc(tp_hi[h], 1)
                    with act.Fori(0, (NCH - 3) // 2) as r:
                        for e in range(2):
                            chunk(r * 2 + (2 + e), 2 + e)
                    c = NCH - 1
                    hi_g(g0 + NCH, 0)
                    hi_d(d0 + c, (d0 + c) % 2)
                    gate(c, 0)
                    hT_high(1, t0 + c - 1 + p_use(s, c - 1, 1))
                    hi_g(g0 + NCH, 1)
                    hT_high(0, t0 + c + p_use(s, c, 0))
                    gate(c, 1)
                    hT_high(1, t0 + c + p_use(s, c, 1), at=2)
                    use = t0 + NCH + p_use(s, c, 0)
                    xT_high(0, use)
                    if k == 0:
                        act.wait_ge(f_loaded, 16)
                        copy(wf_hi[:, :, :], wf_raw[:, :, :]).then_inc(f_hi, 1)

                    def half1(use=use):
                        xT_high(1, use)

                if kind == "ple":
                    for part in range(2):
                        hi_g(g0 + 1, part)
                    hi_d(d0, d0 % 2, free=2 * (d0 - 2) + 3)
                    for n, (j, h) in enumerate(PAIR):
                        if n == 2:
                            half1()
                        act.wait_ge(g_done, 2 * g0 + n + 1)
                        if n >= 2:
                            act.wait_ge(tok_ready, x0 + n - 1)
                        act.activation(stage[:, j, :], gu[j][:, :], ACT.Sigmoid).then_inc(act_done, 1)
                        if n == 2 and not last_phase:
                            hi_g(g0 + 2, 0)
                            xT_high(0, t0)
                            hi_g(g0 + 2, 1)

                    def half1(use=t0):
                        xT_high(1, use)

                if kind == "attn":
                    for e in ATTN_ORDER:
                        if e[0] == "g":
                            c, h = e[1:]
                            hi_g(g0 + c + 1, h)
                            act.wait_ge(g_done, 2 * (g0 + c) + h + 1)
                            if c % 3 == 2:
                                g = c // 3
                                copy(v_att[:, h, 512 * g:512 * g + 512], gu[h][:, :]).then_inc(gu_taken[h], 1)
                            else:
                                if c > 0:
                                    before = {1: 0, 3: 1, 4: 3}[c]
                                    act.wait_ge(tp_full[h], t0 + tp_of[("turn", before, h)][1] + 1)
                                copy(stage[:, h, :], gu[h][:, :], SCALE if c % 3 == 0 else 1.0)\
                                    .then_inc(gu_taken[h], 1)
                        elif e[0] == "half1":
                            half1()
                        elif e[0] == "exp":
                            act.wait_ge(f_arg, 1)
                            act.activation(lf[:, 3, :], lf[:, 2, :], ACT.Exp).then_inc(f_exp, 1)
                        elif e[0] == "log":
                            act.wait_ge(f_arg, 2)
                            act.activation(lf[:, 5, :], lf[:, 4, :], ACT.Ln).then_inc(f_ln, 1)
                        elif e[0] == "head":
                            n = e[1]
                            if n < 2 * HEADS:
                                b = n % 2
                                act.wait_ge(s_taken, n + 1)
                                for q, cols in ((0, slice(0, S)), (1, slice(S, S + P))):
                                    done = act.activation(probs[:, b, cols], logits[:, b, cols], ACT.Exp,
                                                          bias=neg_max[:, b, q:q + 1],
                                                          accum_out=row_sum[:, 1 - q, n:n + 1])
                                done.then_inc(p_ready, 1)
                            if 1 <= n <= 2 * HEADS:
                                b, at = tp_of[("probs", n - 1)]
                                act.wait_ge(tp_full[b], t0 + at + 1)
                                if n >= 3:
                                    act.wait_ge(pv_done, n - 2)
                                copy(probsT[:, b, :], tp[b][:, 0:384]).then_inc(tp_taken[b], 1)
                            if n in (14, 15):
                                h = n - 14
                                act.wait_ge(o_turned, h + 1)
                                copy(xT_hi[:, 0:4, h * P:(h + 1) * P],
                                     acc[1][:, h, :].rearrange("p (b t) -> p b t", b=4)).then_inc(o_hi, 1)
                        elif e[0] == "oT":
                            h = e[1]
                            if h == 0:
                                hi_g(g0 + 7, 0)
                            xT_high_block(1, h, t0 + tp_of[e][1], bank=1 - h)
                    hi_g(g0 + 7, 1)
                    after, end = g0 + 8, t0 + 5 + HEADS + 1

                if kind == "sgu":
                    def gelu(n, dst, cols):
                        act.wait_ge(gu_taken[n % 2], u0 + n // 2 + 1)
                        act.activation(dst[:, cols[0], 512 * cols[1]:512 * cols[1] + 512], stage[:, n % 2, :],
                                       ACT.Gelu_apprx_tanh).then_inc(act_done, 1)

                    hi_g(g0 + 1, 0)
                    half1()
                    gelu(0, v_sgu, (0, 0))
                    hi_g(g0 + 1, 1)
                    hi_g(g0 + 2, 0)
                    gelu(1, v_sgu, (1, 0))
                    hi_g(g0 + 2, 1)
                    act.wait_ge(ws_turned, 1)
                    for b in range(2):
                        done = copy(ws_T[:, 4 * b:4 * b + 4, :], acc[0][:, b, :].rearrange("p (b t) -> p b t", b=4))
                    done.then_inc(ws_taken, 1)
                    gelu(2, v_sgu, (0, 1))
                    gelu(3, v_sgu, (1, 1))
                    hi_g(g0 + 3, 0)
                    hi_g(g0 + 3, 1)
                    gelu(4, u_sgu, (0, 0))
                    gelu(5, u_sgu, (1, 0))
                    hi_g(g0 + 4, 0)
                    gelu(6, u_sgu, (0, 1))
                    hi_g(g0 + 4, 1)
                    xT_high(0, t0)
                    gelu(7, u_sgu, (1, 1))
                    for part in range(2):
                        hi_g(g0 + 5, part)
                    xT_high(1, t0)
                    after, end = g0 + 6, t0 + 2

                if kind in ("attn", "sgu"):
                    hi_g(after, 0)
                    xT_high(0, end)
                    hi_g(after, 1)

                    def half1(use=end):
                        xT_high(1, use)

        @block.vector
        def _(dve):
            steps = [0]

            def link(instruction):
                instruction.then_inc(step, 1)
                steps[0] += 1
                dve.wait_ge(step, steps[0])

            def low(dst, src, hi):
                return dve.tensor_tensor(dst, src, hi.bitcast(F32), ALU.subtract)

            def lo_g_into(n, slot, part):
                raw, high, done = ((rawA, high_a, split_a), (rawB, high_b, split_b))[part]
                ks = slice(4 * part, 4 * part + 4)
                dve.wait_ge(high, n + 1)
                low(g_lo[:, slot, ks, :], raw[:, :, :], g_hi[:, slot, ks, :]).then_inc(done, 1)

            def lo_g(n, part):
                lo_g_into(n, n % 2, part)

            def lo_d(m, slot):
                dve.wait_ge(high_d, m + 1)
                low(d_lo[:, slot, :, :], rawD[:, :, :], d_hi[:, slot, :, :]).then_inc(split_d, 1)

            def xT_low(h, use):
                for j in range(2):
                    xT_low_block(j, h, use + h, bank=j)

            def xT_low_block(j, h, use, bank):
                dve.wait_ge(tp_hi[bank], use + 1)
                part = (slice(None), slice(4 * j, 4 * j + 4), slice(h * P, (h + 1) * P))
                low(xT_lo[part], tp[bank][:, :].rearrange("p (b t) -> p b t", b=4), xT_hi[part])\
                    .then_inc(tp_taken[bank], 1)

            def hT_low(h, use, at=None):
                at = h if at is None else at
                dve.wait_ge(tp_hi[h], use + 1)
                low(hT_lo[:, at, :, :], tp[h][:, 0:2 * P].rearrange("p (b t) -> p b t", b=2), hT_hi[:, at, :, :])\
                    .then_inc(tp_taken[h], 1)

            def ln_moments(h, done):
                link(done)
                link(dve.bn_aggr(mean_var[:, h, :], stats[:, h, :]))
                dve.tensor_scalar(var_eps[:, h:h + 1], mean_var[:, h, 1:2], EPS, None, ALU.add)\
                    .then_inc(var_ready, 1)

            def ln_stats(src, h):
                for j in range(2):
                    done = dve.bn_stats(stats[:, h, 6 * j:6 * j + 6], src[:, 512 * j:512 * j + 512])
                ln_moments(h, done)

            def ln_apply(src, dst, h, ln, j, ready):
                if j == 0 and h == 0:
                    dve.wait_ge(ln_loaded, 32 * (ln + 1))
                cols = slice(512 * j, 512 * j + 512)
                link(dve.scalar_tensor_tensor(out=src[:, cols], in0=src[:, cols], scalar=mean_var[:, h, 0:1],
                                              in1=gamma[:, cols], op0=ALU.subtract, op1=ALU.mult))
                if j == 0:
                    dve.wait_ge(rstd_ready, 2 * ln + h + 1)
                dve.scalar_tensor_tensor(out=dst[:, cols], in0=src[:, cols], scalar=rstd[:, h:h + 1],
                                         in1=beta[:, cols], op0=ALU.mult, op1=ALU.add).then_inc(ready, 1)

            def residual(h, j, r0, done):
                dve.wait_ge(*done)
                cols = slice(512 * j, 512 * j + 512)
                dve.scalar_tensor_tensor(out=t_tok[:, h, cols], in0=x_tok[:, h, cols], scalar=ALPHA,
                                         in1=acc[h][:, j, :], op0=ALU.mult, op1=ALU.add).then_inc(acc_read, 1)
                dve.wait_ge(acc_read, r0 + 2 * h + j + 1)
                return dve.bn_stats(stats[:, h, 6 * j:6 * j + 6], t_tok[:, h, cols])

            def x_apply(h, ln, j):
                ln_apply(t_tok[:, h, :], x_tok[:, h, :], h, ln, j, tok_ready)

            def norm_half1(r0, ln, done, use):
                def apply():
                    for j in range(2):
                        x_apply(1, ln, j)
                return lambda: ln_moments(1, residual(1, 1, r0, done)), apply, lambda: xT_low(1, use)

            xT_low(0, 0)
            dve.wait_ge(high_q, 1)
            low(g_lo[:, 0, 0:2, :], rawA[:, 0:2, :], g_hi[:, 0, 0:2, :]).then_inc(split_q, 1)
            dve.wait_ge(high_a, 1)
            low(g_lo[:, 0, 2:4, :], rawA[:, 2:4, :], g_hi[:, 0, 2:4, :]).then_inc(split_a, 1)
            lo_g(0, 1)
            light = True

            half1_steps = (lambda: xT_low(1, 0),)

            def half1():
                for part in half1_steps:
                    part()

            for k, (kind, i, s) in enumerate(PHASES):
                B = bases[k]
                f0 = sum(kind in ("ffn", "ple") for kind, _, _ in PHASES[:k])
                g0, d0, u0, t0, v0, a0, x0, r0, ln0 = (B[q] for q in ("g", "d", "u", "t", "v", "a", "x", "r", "ln"))
                last_phase = k + 1 == len(PHASES)

                if kind == "ffn":
                    def gated(c, h):
                        dve.wait_ge(act_done, 2 * c + (a0 + h + 1))
                        dve.scalar_tensor_tensor(out=stage[:, h, FC:2 * FC], in0=stage[:, h, 0:FC], scalar=0.5,
                                                 in1=gu[h][:, FC:2 * FC], op0=ALU.mult, op1=ALU.mult)\
                            .then_inc(gu_taken[h], 1)

                    def chunk(c, cs):
                        slot = (g0 + cs + 1) % 2
                        if cs == 0 and not light:
                            half1()
                            gated(c, 0)
                        if k == 0 and cs == 0:
                            half1()
                        lo_g_into(c + (g0 + 1), slot, 0)
                        if cs == 0 and light:
                            if k > 0:
                                half1()
                            gated(c, 0)
                        if cs > 0:
                            gated(c, 0)
                            hT_low(1, c + (v0 - 1 + p_use(s, cs - 1, 1)))
                        lo_d(c + d0, (d0 + cs) % 2)
                        lo_g_into(c + (g0 + 1), slot, 1)
                        gated(c, 1)
                        hT_low(0, c + (v0 + p_use(s, cs, 0)))

                    chunk(0, 0)
                    if k == 0:
                        dve.wait_ge(bias_mm, 1)
                        link(dve.tensor_copy(bias_row_sb, acc[1][0:HEADS, 1, :]))
                        dve.memset(bias_row_sb[:, S:512], NEG).then_inc(bias_sb, 1)
                    chunk(1, 1)
                    if s == 2:
                        for h in range(HALVES):
                            dve.wait_ge(tp_hi[h], v0 + 3 - h)
                            low(pT_lo[:, h, :, :], tp[h][:, 0:2 * P].rearrange("p (b t) -> p b t", b=2),
                                pT_hi[:, h, :, :]).then_inc(tp_taken[h], 1)
                    with dve.Fori(0, (NCH - 3) // 2) as r:
                        for e in range(2):
                            chunk(r * 2 + (2 + e), 2 + e)
                    c = NCH - 1
                    lo_g(g0 + NCH, 0)
                    lo_d(d0 + c, (d0 + c) % 2)
                    gated(c, 0)
                    hT_low(1, v0 + c - 1 + p_use(s, c - 1, 1))
                    hT_low(0, v0 + c + p_use(s, c, 0))
                    lo_g(g0 + NCH, 1)
                    residual(0, 0, r0, (d_first, 2 * f0 + 1))
                    ln_moments(0, residual(0, 1, r0, (d_done, 2 * (d0 + c))))
                    x_apply(0, ln0, 0)
                    gated(c, 1)
                    x_apply(0, ln0, 1)
                    hT_low(1, v0 + c + p_use(s, c, 1), at=2)
                    use = v0 + NCH + p_use(s, c, 0)
                    xT_low(0, use)
                    residual(1, 0, r0, (d_first, 2 * f0 + 2))
                    if k == 0:
                        dve.wait_ge(f_hi, 1)
                        low(wf_lo[:, :, :], wf_raw[:, :, :], wf_hi[:, :, :]).then_inc(f_split, 1)
                    light = False
                    half1_steps = norm_half1(r0, ln0, (d_done, 2 * (d0 + NCH)), use)

                if kind == "ple":
                    stats_1, apply_1, low_1 = half1_steps
                    stats_1()
                    lo_g(g0 + 1, 0)
                    lo_g(g0 + 1, 1)
                    apply_1()
                    lo_d(d0, d0 % 2)
                    low_1()
                    for n, (j, h) in enumerate(PAIR):
                        cols = slice(512 * j, 512 * j + 512)
                        if n == 2 and not last_phase:
                            lo_g(g0 + 2, 0)
                        if n % 2 == 0:
                            dve.wait_ge(d_done, 2 * d0 + h + 1)
                        dve.wait_ge(act_done, a0 + n + 1)
                        dve.tensor_tensor(stage[:, j, :], stage[:, j, :], acc[h][:, j, :], ALU.mult)\
                            .then_inc(gu_taken[j], 1)
                        dve.wait_ge(gu_taken[j], u0 + n // 2 + 1)
                        dve.tensor_tensor(x_tok[:, h, cols], x_tok[:, h, cols], stage[:, j, :], ALU.add)\
                            .then_inc(tok_ready, 1)
                        if n == 2 and not last_phase:
                            xT_low(0, v0)
                            lo_g(g0 + 2, 1)
                    light = True
                    half1_steps = (lambda use=v0: xT_low(1, use),)

                if kind == "attn":
                    def group_out(g, halves=(0, 1)):
                        cols = slice(HEADS * g, HEADS * g + HEADS)
                        if 0 in halves:
                            dve.wait_ge(pv_done, HEADS * (g + 1))
                            link(dve.reciprocal(row_inv[:, :, cols], row_sum[:, :, cols]))
                        for q in halves:
                            dve.tensor_tensor(
                                t_tok[:, q, 512 * g:512 * g + 512].rearrange("p (n d) -> p n d", d=HD),
                                heads_out[g][q].rearrange("p (n d) -> p n d", d=HD),
                                row_inv[:, q, cols].unsqueeze(2).to_broadcast([P, HEADS, HD]),
                                ALU.mult).then_inc(tok_ready, 1)

                    half1()
                    for e in ATTN_ORDER:
                        if e[0] == "g":
                            lo_g(g0 + e[1] + 1, e[2])
                        elif e[0] == "turn":
                            c, h = e[1:]
                            dst, g, at = (qT, kT)[c % 3], c // 3, tp_of[e][1]
                            dve.wait_ge(tp_full[h], t0 + at + 1)
                            dve.tensor_copy(dst[:, 4 * g:4 * g + 4, h * P:(h + 1) * P],
                                            tp[h][:, :].rearrange("p (b t) -> p b t", b=4)).then_inc(tp_taken[h], 1)
                        elif e[0] == "forget":
                            dve.wait_ge(rows_loaded, 32)
                            dve.wait_ge(f_mm, 1)
                            link(dve.tensor_scalar(lf[:, 6, :], acc[0][0:HEADS, 0, 0:S], bf_col, None, ALU.add))
                            link(dve.tensor_scalar(lf[:, 7, :], lf[:, 6, :], -1.0, None, ALU.mult))
                            dve.tensor_tensor(lf[:, 2, :], lf[:, 6, :], lf[:, 7, :], ALU.min).then_inc(f_arg, 1)
                        elif e[0] == "flip":
                            dve.wait_ge(bias_flip, 1)
                            for q in range(4):
                                done = dve.tensor_copy(bias_tab[:, 512 * q:512 * q + 512],
                                                       acc[q // 2][:, q % 2, :])
                            done.then_inc(bias_done, 1)
                        elif e[0] == "exp":
                            dve.wait_ge(f_exp, 1)
                            link(dve.tensor_scalar(lf[:, 4, :], lf[:, 3, :], 1.0, None, ALU.add))
                            dve.tensor_scalar(lf[:, 7, :], lf[:, 4, :], -1.0, None, ALU.add).then_inc(f_arg, 1)
                            link(dve.reciprocal(lf[:, 0, :], lf[:, 4, :]))
                            dve.wait_ge(f_arg, 2)
                            link(dve.tensor_tensor(lf[:, 7, :], lf[:, 3, :], lf[:, 7, :], ALU.subtract))
                            link(dve.tensor_tensor(lf[:, 7, :], lf[:, 7, :], lf[:, 0, :], ALU.mult))
                            link(dve.memset(lf[:, 2, :], 1.0))
                        elif e[0] == "log":
                            dve.wait_ge(f_ln, 1)
                            link(dve.tensor_tensor(lf[:, 5, :], lf[:, 5, :], lf[:, 7, :], ALU.add))
                            link(dve.tensor_scalar(lf[:, 7, :], lf[:, 6, :], 0.0, None, ALU.min))
                            link(dve.tensor_tensor(lf[:, 7, :], lf[:, 7, :], lf[:, 5, :], ALU.subtract))
                            link(dve.tensor_tensor_scan(lf[:, 0, :], lf[:, 2, :], lf[:, 7, :], 0.0,
                                                        ALU.mult, ALU.add))
                            link(dve.tensor_scalar(lf[:, 1, :], lf[:, 0, :], -1.0, None, ALU.mult))
                            keys = ((slice(0, S), slice(0, S)), (slice(S, S + P), slice(0, P)))
                            for cols, src in keys:
                                done = dve.tensor_copy(c_hi[:, cols], lf[:, 1, src])
                            link(done)
                            for cols, src in keys:
                                done = low(c_lo[:, cols], lf[:, 1, src], c_hi[:, cols])
                            done.then_inc(f_cum, 1)
                        elif e[0] == "cT":
                            for h in range(HALVES):
                                dve.wait_ge(tp_full[h], t0 + tp_of[("cT", h)][1] + 1)
                                dve.tensor_copy(c_tok[:, h, :], tp[h][:, 0:HEADS]).then_inc(tp_taken[h], 1)
                        elif e[0] == "head":
                            n = e[1]
                            if n < 2 * HEADS:
                                g, hh, b = n // HEADS, n % HEADS, n % 2
                                pieces = ((0, slice(0, S), 0), (1, slice(S, S + P), P))
                                if n == 0:
                                    dve.wait_ge(bias_done, 1)
                                if n == HEADS:
                                    for h in range(HALVES):
                                        dve.wait_ge(tp_taken[h], t0 + tp_of[("cT", h)][1] + 1)
                                if g == 1:
                                    for q, cols, at in pieces:
                                        done = dve.tensor_scalar(causal_c[:, b, cols], causal[:, at:S],
                                                                 c_tok[:, 1 - q, hh:hh + 1], None, ALU.add)
                                    link(done)
                                dve.wait_ge(s_full, n + 1)
                                if n >= 2:
                                    dve.wait_ge(p_ready, n - 1)
                                for q, cols, at in pieces:
                                    add = (causal_c[:, b, cols] if g == 1
                                           else bias_tab[:, S * hh + at:S * hh + S])
                                    done = dve.tensor_tensor_reduce(
                                        out=logits[:, b, cols], in0=acc[0][:, b, cols], in1=add, scale=1.0,
                                        scalar=-3.0e38, op0=ALU.add, op1=ALU.max,
                                        accum_out=row_max[:, b, q:q + 1])
                                link(done)
                                dve.tensor_scalar(neg_max[:, b, :], row_max[:, b, :], -1.0, None, ALU.mult)\
                                    .then_inc(s_taken, 1)
                            if n in (HEADS + 2, HEADS + 3):
                                group_out(0, (n - HEADS - 2,))
                            if n in (15, 16):
                                h = n - 15
                                dve.wait_ge(o_hi, h + 1)
                                part = (slice(None), slice(0, 4), slice(h * P, (h + 1) * P))
                                low(xT_lo[part], acc[1][:, h, :].rearrange("p (b t) -> p b t", b=4), xT_hi[part])\
                                    .then_inc(o_split, 1)
                        elif e[0] == "oT":
                            h = e[1]
                            if h == 0:
                                group_out(1)
                            xT_low_block(1, h, v0, bank=1 - h)
                            if h == 0:
                                lo_g(g0 + 7, 0)
                    lo_g(g0 + 7, 1)
                    out0, end = g0 + 6, v0 + 1

                if kind == "sgu":
                    def biased(n, c):
                        at = 512 * SGU_ORDER[c]
                        dve.wait_ge(g_done, 2 * g0 + n + 1)
                        if n >= 2:
                            dve.wait_ge(act_done, a0 + n - 1)
                        dve.tensor_tensor(stage[:, n % 2, :], gu[n % 2][:, :], bias_tab[:, at:at + 512], ALU.add)\
                            .then_inc(gu_taken[n % 2], 1)

                    def gate_y(h):
                        dve.wait_ge(mix_done, h + 1)
                        dve.wait_ge(act_done, a0 + 7 + h)
                        for g in range(HEADS):
                            cols = slice(P * g, P * g + P)
                            done = dve.scalar_tensor_tensor(
                                out=t_tok[:, h, cols], in0=acc[h][:, g // 4, P * (g % 4):P * (g % 4) + P],
                                scalar=bs_col[:, g:g + 1], in1=u_sgu[:, h, cols], op0=ALU.add, op1=ALU.mult)
                            if g % 4 == 3:
                                done.then_inc(tok_ready, 1)

                    half1()
                    dve.wait_ge(sgu_bias_ld, 16)
                    lo_g(g0 + 1, 0)
                    biased(0, 0)
                    lo_g(g0 + 1, 1)
                    biased(1, 0)
                    lo_g(g0 + 2, 0)
                    biased(2, 1)
                    lo_g(g0 + 2, 1)
                    dve.wait_ge(act_done, a0 + 3)
                    ln_stats(v_sgu[:, 0, :], 0)
                    biased(3, 1)
                    for j in range(2):
                        ln_apply(v_sgu[:, 0, :], v_sgu[:, 0, :], 0, ln0, j, vn_ready)
                    dve.wait_ge(act_done, a0 + 4)
                    ln_stats(v_sgu[:, 1, :], 1)
                    lo_g(g0 + 3, 0)
                    biased(4, 2)
                    lo_g(g0 + 3, 1)
                    for j in range(2):
                        ln_apply(v_sgu[:, 1, :], v_sgu[:, 1, :], 1, ln0, j, vn_ready)
                    biased(5, 2)
                    biased(6, 3)
                    lo_g(g0 + 4, 0)
                    gate_y(0)
                    lo_g(g0 + 4, 1)
                    biased(7, 3)
                    xT_low(0, v0)
                    gate_y(1)
                    for part in range(2):
                        lo_g(g0 + 5, part)
                    xT_low(1, v0)
                    ln0, out0, end = ln0 + 1, g0 + 4, v0 + 2

                if kind in ("attn", "sgu"):
                    residual(0, 0, r0, (g_done, 2 * out0 + 1))
                    ln_moments(0, residual(0, 1, r0, (g_done, 2 * out0 + 2)))
                    for j in range(2):
                        x_apply(0, ln0, j)
                    residual(1, 0, r0, (g_done, 2 * out0 + 3))
                    lo_g(out0 + 2, 0)
                    xT_low(0, end)
                    lo_g(out0 + 2, 1)
                    light = False
                    half1_steps = norm_half1(r0, ln0, (g_done, 2 * out0 + 4), end)

        @block.gpsimd
        def _(pool):
            pool.memset(ident[:, :], 0.0).then_inc(pool_step, 1)
            pool.wait_ge(pool_step, 1)
            pool.affine_select(out=ident[:, :], in_=ident[:, :], compare_op=ALU.not_equal, fill=1.0, base=0,
                               pattern=[[-1, P]], channel_multiplier=1).then_inc(const_ready, 1)
            pool.memset(flip[:, :], 0.0).then_inc(pool_step, 1)
            pool.wait_ge(pool_step, 2)
            pool.affine_select(out=flip[:, :], in_=flip[:, :], compare_op=ALU.not_equal, fill=1.0, base=1 - P,
                               pattern=[[1, P]], channel_multiplier=1).then_inc(const_ready, 1)
            pool.dma_start(rel_sb[:, :], rel_bias).then_inc(bias_in, 16)
            pool.dma_start(onehot_sb, bucket_onehot).then_inc(bias_in, 16)
            pool.memset(neg_half, -0.5).then_inc(pool_step, 1)

            def load_ln(ln):
                g, b = [(ln_g[i, s], ln_b[i, s]) for i, s in ((0, 0), (0, 1), (0, 2), (1, 0))][ln] if ln < 4 \
                    else ((sgu_ln_g[0], sgu_ln_b[0]), (ln_g[1, 1], ln_b[1, 1]), (ln_g[1, 2], ln_b[1, 2]))[ln - 4]
                for dst, src in ((gamma, g), (beta, b)):
                    pool.dma_start(dst[:, :], src.partition_broadcast(P)).then_inc(ln_loaded, 16)

            pool.wait_ge(split_a, 2)
            load_ln(0)
            with nc.allow_non_contiguous_dma(reason="eight columns, once"):
                pool.dma_start(wf_raw[:, :, :], attn_w_in[0].rearrange("(b p) n -> p b n", p=P)
                               [:, :, 6 * 512:6 * 512 + HEADS]).then_inc(f_loaded, 16)
                pool.dma_start(bs_col, sgu_b_s[0].rearrange("g t -> t g")).then_inc(rows_loaded, 16)
            pool.dma_start(bf_col, attn_b_f.rearrange("o n -> n o")).then_inc(rows_loaded, 16)
            pool.dma_start(p_tok[:, :, :], p_in[0, 0].rearrange("(h p) n -> p h n", p=P)).then_inc(p_loaded, 16)
            pool.memset(causal[:, :], 0.0).then_inc(pool_step, 1)
            pool.memset(sel_r[:, :].bitcast(F32), 0.0).then_inc(pool_step, 1)
            pool.wait_ge(pool_step, 5)
            pool.affine_select(out=causal[:, :], in_=causal[:, :], compare_op=ALU.is_ge, fill=NEG, base=P,
                               pattern=[[-1, S]], channel_multiplier=1).then_inc(const_ready, 1)
            sel_v = sel_r[:, :].rearrange("p (n t) -> p n t", t=P)
            pool.affine_select(out=sel_v, in_=sel_v.bitcast(F32), compare_op=ALU.not_equal, fill=1.0, base=0,
                               pattern=[[-1, HEADS], [0, P]], channel_multiplier=1).then_inc(const_ready, 1)
            pool.wait_ge(bias_sb, 1)
            pool.dma_start(bias_rows, bias_row_sb).then_inc(bias_st, 16)
            pool.wait_ge(bias_st, 16)
            ln_end = []
            for k, (kind, _, _) in enumerate(PHASES):
                if kind == "ffn":
                    ln_end.append((tok_ready, bases[k]["x"] + 4))
                elif kind == "sgu":
                    ln_end.append((vn_ready, 4))
                if kind in ("attn", "sgu"):
                    ln_end.append((tok_ready, bases[k]["x"] + 8))
            for ln in range(total["ln"]):
                for h in range(HALVES):
                    pool.wait_ge(var_ready, 2 * ln + h + 1)
                    pool.tensor_tensor(rstd[:, h:h + 1], var_eps[:, h:h + 1], neg_half, ALU.pow)\
                        .then_inc(rstd_ready, 1)
                    if ln == 3 and h == 0:
                        pool.wait_ge(d_done, 2 * (bases[4]["d"] + NCH))
                        pool.dma_start(ws_tok[:, :, :], sgu_w_s[0].rearrange("g t s -> t g s")).then_inc(ws_raw, 16)
                    if ln == 0 and h == 0:
                        pool.wait_ge(d_done, 2 * NCH)
                        pool.dma_start(bias_rev[:, :, :].rearrange("p h (n u) -> p (h n) u", u=S),
                                       bass.AP(bias_rows.tensor, 0, [[1, P], [512, HEADS], [1, S]]))\
                            .then_inc(bias_ld, 16)
                if ln == 2:
                    pool.dma_start(bias_tab[:, :], sgu_b_in[0].partition_broadcast(P)).then_inc(sgu_bias_ld, 16)
                if ln == 3:
                    pool.wait_ge(ws_raw, 16)
                    pool.affine_select(out=ws_tok[:, :, :], in_=ws_tok[:, :, :], compare_op=ALU.is_ge, fill=0.0,
                                       base=0, pattern=[[0, HEADS], [-1, P]], channel_multiplier=1)\
                        .then_inc(ws_loaded, 1)
                    pool.dma_start(p_tok[:, :, :], p_in[1, 0].rearrange("(h p) n -> p h n", p=P))\
                        .then_inc(p_loaded, 16)
                if ln + 1 < total["ln"]:
                    pool.wait_ge(*ln_end[ln])
                    load_ln(ln + 1)


def bucket_of(n):
    exact = BUCKETS // 2
    if n < exact:
        return n
    big = exact + int(np.float32(np.log(np.float32(n / exact))) / np.float32(math.log(128 / exact))
                      * np.float32(BUCKETS - exact))
    return min(big, BUCKETS - 1)


_INS = ["x", "p", "ln_g", "ln_b", "ffn_w_gate", "ffn_w_up", "ffn_w_down", "attn_w_in", "attn_b_f", "attn_w_out",
        "rel_bias", "sgu_w_in", "sgu_b_in", "sgu_ln_g", "sgu_ln_b", "sgu_w_s", "sgu_b_s", "sgu_w_out",
        "ple_w_proj", "ple_w_gate"]


def kernel(**inputs):
    import concourse.bacc as bacc
    from concourse.bass_utils import run_bass_kernel_spmd

    nc = bacc.Bacc("TRN2", target_bir_lowering=False, num_devices=1)
    onehot = np.zeros((BUCKETS, 512), np.float32)
    for j in range(S):
        onehot[bucket_of(S - 1 - j), j] = 1.0
    arrays = {"in_bucket_onehot": onehot}
    args = [nc.dram_tensor("in_bucket_onehot", onehot.shape, F32, kind="ExternalInput").ap()]
    for name in _INS:
        a = np.ascontiguousarray(inputs[name])
        arrays[f"in_{name}"] = a
        args.append(nc.dram_tensor(f"in_{name}", a.shape, mybir.dt.from_np(a.dtype), kind="ExternalInput").ap())
    out = nc.dram_tensor("out_0", (1, S, D), F32, kind="ExternalOutput").ap()
    build(nc, *args, out)
    r = run_bass_kernel_spmd(nc, [arrays], core_ids=[0])
    return r.results[0]["out_0"]
```
